# Optimizing a Trainium2 kernel written in Bass

```python
import jax, jax.numpy as jnp
from jax import lax
import numpy as np
import math
import jax
import jax.numpy as jnp

D_MODEL = 1024
BATCH = 1
SEQ = 512
DEPTH = 1

CHUNK = 64
Q_BLOCK = 128

GDN_HEADS = 4
GDN_HEAD_DIM = 128
GDN_WIDTH = GDN_HEADS * GDN_HEAD_DIM
GDN_CONV = 4
SB_HEADS = 8
SB_HEAD_DIM = 64
SB_WIDTH = SB_HEADS * SB_HEAD_DIM
SC_GROUPS = 8
SC_WIDTH = 512
SC_CONV = 3
N_BRANCH = 3
BRANCH_WIDTH = 512
D_FF = 4 * D_MODEL
EPS = 1e-6

_SIZES = (3 * GDN_WIDTH,
          GDN_WIDTH,
          GDN_HEADS,
          GDN_HEADS,
          3 * SB_WIDTH,
          SC_WIDTH,
          SC_WIDTH,
          SC_WIDTH,
          N_BRANCH * D_MODEL)
IN_PROJ_WIDTH = sum(_SIZES)
SPLIT_POINTS = tuple(int(s) for s in np.cumsum(_SIZES)[:-1])


def rms_norm(x, w):
    x32 = x.astype(jnp.float32)
    y = x32 * lax.rsqrt(jnp.mean(x32 * x32, axis=-1, keepdims=True) + EPS)
    return (y * w.astype(jnp.float32)).astype(x.dtype)

def l2_normalize(x):
    return x * lax.rsqrt(jnp.sum(x * x, axis=-1, keepdims=True) + EPS)

def causal_depthwise_conv(x, w):
    k_len, ch = w.shape
    return lax.conv_general_dilated(
        x, w.astype(x.dtype)[:, None, :], window_strides=(1,), padding=[(k_len - 1, 0)],
        dimension_numbers=("NWC", "WIO", "NWC"), feature_group_count=ch)

def gated_delta_rule(q, k, v, g, beta):
    bsz, seq, heads, dk = q.shape
    dv = v.shape[-1]
    n_chunks = seq // CHUNK

    def chunkify(t):
        return jnp.moveaxis(t.reshape((bsz, n_chunks, CHUNK) + t.shape[2:]), 3, 2)

    q, k, v, g, beta = (chunkify(t) for t in (q, k, v, g, beta))
    g = jnp.cumsum(g, axis=-1)
    tri = jnp.tril(jnp.ones((CHUNK, CHUNK), dtype=bool))
    strict = jnp.tril(jnp.ones((CHUNK, CHUNK), dtype=bool), k=-1)
    decay = jnp.exp(jnp.where(tri, g[..., :, None] - g[..., None, :], -jnp.inf))

    k_beta = k * beta[..., None]
    v_beta = v * beta[..., None]
    a_kk = jnp.where(strict, jnp.einsum("bnhcd,bnhed->bnhce", k_beta, k) * decay, 0.0)
    lhs = a_kk + jnp.eye(CHUNK, dtype=a_kk.dtype)
    rhs = jnp.concatenate([v_beta, k_beta * jnp.exp(g)[..., None]], axis=-1)
    sol = lax.linalg.triangular_solve(lhs, rhs, left_side=True, lower=True, unit_diagonal=True)
    u, w = sol[..., :dv], sol[..., dv:]

    a_qk = jnp.where(tri, jnp.einsum("bnhcd,bnhed->bnhce", q, k) * decay, 0.0)
    q_dec = q * jnp.exp(g)[..., None]
    k_dec = k * jnp.exp(g[..., -1:] - g)[..., None]
    g_last = jnp.exp(g[..., -1])

    def step(state, inp):
        q_c, k_c, u_c, w_c, a_c, gl_c = inp
        v_new = u_c - jnp.einsum("bhcd,bhde->bhce", w_c, state)
        o_c = (jnp.einsum("bhcd,bhde->bhce", q_c, state)
               + jnp.einsum("bhcs,bhse->bhce", a_c, v_new))
        state = state * gl_c[..., None, None] + jnp.einsum("bhcd,bhce->bhde", k_c, v_new)
        return state, o_c

    xs = tuple(jnp.moveaxis(t, 1, 0) for t in (q_dec, k_dec, u, w, a_qk, g_last))
    state0 = jnp.zeros((bsz, heads, dk, dv), jnp.float32)
    _, o = lax.scan(step, state0, xs)
    return o.transpose(1, 0, 3, 2, 4).reshape(bsz, seq, heads, dv)

def gdn_branch(qkv, gate, a, b, conv_w, a_log, dt_bias, norm_w):
    bsz, seq, _ = qkv.shape
    out_dtype = qkv.dtype
    qkv = jax.nn.silu(causal_depthwise_conv(qkv, conv_w)).astype(jnp.float32)
    q, k, v = jnp.split(qkv, 3, axis=-1)
    shp = (bsz, seq, GDN_HEADS, GDN_HEAD_DIM)
    q = l2_normalize(q.reshape(shp)) * (GDN_HEAD_DIM ** -0.5)
    k = l2_normalize(k.reshape(shp))
    v = v.reshape(shp)
    beta = jax.nn.sigmoid(b.astype(jnp.float32))
    g = -jnp.exp(a_log.astype(jnp.float32)) * jax.nn.softplus(a.astype(jnp.float32) + dt_bias.astype(jnp.float32))
    o = gated_delta_rule(q, k, v, g, beta)
    o = o * lax.rsqrt(jnp.mean(o * o, axis=-1, keepdims=True) + EPS) * norm_w.astype(jnp.float32)
    o = o * jax.nn.silu(gate.astype(jnp.float32).reshape(shp))
    return o.reshape(bsz, seq, GDN_WIDTH).astype(out_dtype)

def stick_breaking_branch(qkv):
    bsz, seq, _ = qkv.shape
    q, k, v = jnp.split(qkv, 3, axis=-1)
    shp = (bsz, seq, SB_HEADS, SB_HEAD_DIM)
    q, k, v = q.reshape(shp), k.reshape(shp), v.reshape(shp)
    scale = SB_HEAD_DIM ** -0.5
    outs = []
    for blk in range(seq // Q_BLOCK):
        q0 = blk * Q_BLOCK
        k_len = q0 + Q_BLOCK
        z = jnp.einsum("bqhd,bkhd->bhqk", q[:, q0:k_len], k[:, :k_len]).astype(jnp.float32) * scale
        t_idx = q0 + jnp.arange(Q_BLOCK)
        s_idx = jnp.arange(k_len)
        mask = s_idx[None, :] < t_idx[:, None]
        log_1m = jnp.where(mask, jax.nn.log_sigmoid(-z), 0.0)
        after = lax.cumsum(log_1m, axis=3, reverse=True) - log_1m
        att = jnp.where(mask, jnp.exp(jax.nn.log_sigmoid(z) + after), 0.0)
        outs.append(jnp.einsum("bhqk,bkhd->bqhd", att.astype(v.dtype), v[:, :k_len]))
    return jnp.concatenate(outs, axis=1).reshape(bsz, seq, SB_WIDTH)

def short_conv_branch(xin, gate_b, gate_c, conv_w):
    return gate_b * causal_depthwise_conv(gate_c * xin, conv_w)

def first_inputs(seed: int = 0) -> dict:
    key = jax.random.key(seed)
    ks = jax.random.split(key, 16)
    f32 = jnp.float32

    def normal(k, shape, scale):
        return jax.random.normal(k, shape, f32) * scale

    def gain(k):
        return 1.0 + 0.02 * jax.random.normal(k, (DEPTH, D_MODEL), f32)

    dt = jnp.exp(jax.random.uniform(ks[5], (DEPTH, GDN_HEADS), f32, np.log(1e-3), np.log(1e-1)))
    return {
        "x": jax.random.normal(ks[0], (BATCH, SEQ, D_MODEL), f32),
        "norm_mix_pre": gain(ks[1]),
        "w_in": normal(ks[2], (DEPTH, D_MODEL, IN_PROJ_WIDTH), D_MODEL ** -0.5),
        "conv_qkv_w": normal(ks[3], (DEPTH, GDN_CONV, 3 * GDN_WIDTH), GDN_CONV ** -0.5),
        "gdn_a_log": jnp.log(jax.random.uniform(ks[4], (DEPTH, GDN_HEADS), f32, 1.0, 16.0)),
        "gdn_dt_bias": dt + jnp.log(-jnp.expm1(-dt)),
        "gdn_norm_w": 1.0 + 0.02 * jax.random.normal(ks[6], (DEPTH, GDN_HEAD_DIM), f32),
        "conv_sc_w": normal(ks[7], (DEPTH, SC_CONV, SC_WIDTH), SC_CONV ** -0.5),
        "w_branch": normal(ks[8], (DEPTH, N_BRANCH, BRANCH_WIDTH, D_MODEL), BRANCH_WIDTH ** -0.5),
        "w_out": normal(ks[9], (DEPTH, D_MODEL, D_MODEL), D_MODEL ** -0.5),
        "norm_mix_post": gain(ks[10]),
        "norm_ffn_pre": gain(ks[11]),
        "w_ff1": normal(ks[12], (DEPTH, D_MODEL, D_FF), D_MODEL ** -0.5),
        "w_ff2": normal(ks[13], (DEPTH, D_FF, D_MODEL), D_FF ** -0.5),
        "norm_ffn_post": gain(ks[14]),
    }

def first_block(x, norm_mix_pre, w_in, conv_qkv_w, gdn_a_log, gdn_dt_bias, gdn_norm_w, conv_sc_w,
              w_branch, w_out, norm_mix_post, norm_ffn_pre, w_ff1, w_ff2, norm_ffn_post):
    bsz, seq, _ = x.shape
    for l in range(DEPTH):
        h = rms_norm(x, norm_mix_pre[l])
        proj = h @ w_in[l]
        (gdn_qkv, gdn_gate, gdn_a, gdn_b, sb_qkv, sc_x, sc_b, sc_c, gates) = jnp.split(
            proj, SPLIT_POINTS, axis=-1)
        y_a = gdn_branch(gdn_qkv, gdn_gate, gdn_a, gdn_b, conv_qkv_w[l], gdn_a_log[l],
                         gdn_dt_bias[l], gdn_norm_w[l])
        y_b = stick_breaking_branch(sb_qkv)
        y_c = short_conv_branch(sc_x, sc_b, sc_c, conv_sc_w[l])
        gates = jax.nn.sigmoid(gates.reshape(bsz, seq, N_BRANCH, D_MODEL))
        merged = (gates[:, :, 0] * (y_a @ w_branch[l, 0])
                  + gates[:, :, 1] * (y_b @ w_branch[l, 1])
                  + gates[:, :, 2] * (y_c @ w_branch[l, 2]))
        x = x + rms_norm(merged @ w_out[l], norm_mix_post[l])
        h = rms_norm(x, norm_ffn_pre[l])
        f = jnp.square(jax.nn.relu(h @ w_ff1[l])) @ w_ff2[l]
        x = x + rms_norm(f, norm_ffn_post[l])
    return x


DEPTH_2 = 2

N_A_LAYERS = max(1, DEPTH_2 // 2)
N_B_LAYERS = DEPTH_2 - N_A_LAYERS

SSM_GROUP = 16
SSM_GROUPS = D_MODEL // SSM_GROUP
SSM_STATE = 64
STEP_MIN = 1e-3
STEP_MAX = 1e-1

N_HEADS = 16
QK_NOPE_DIM = 64
QK_ROPE_DIM = 32
QK_DIM = QK_NOPE_DIM + QK_ROPE_DIM
V_DIM = 64
Q_LORA_RANK = 384
KV_LORA_RANK = 256
ROPE_THETA = 10000.0

D_FF_2 = -(-8 * D_MODEL // (3 * 256)) * 256

NEG_INF = -1e30


def rms_norm_2(x, gain):
    xf = x.astype(jnp.float32)
    y = xf * lax.rsqrt(jnp.mean(xf * xf, axis=-1, keepdims=True) + EPS)
    return (y * gain.astype(jnp.float32)).astype(x.dtype)

def swiglu_ffn(h, w_gate_up, w_down):
    gate, up = jnp.split(h @ w_gate_up, 2, axis=-1)
    return (jax.nn.silu(gate) * up) @ w_down

def cmul(ar, ai, br, bi):
    return ar * br - ai * bi, ar * bi + ai * br

def s5_mixer(h, w_in, lam_re, lam_im, log_step, b_re, b_im, c_re, c_im, d_skip, w_glu):
    bsz, seq, _ = h.shape
    f32 = jnp.float32
    u = (h @ w_in).reshape(bsz, seq, SSM_GROUPS, SSM_GROUP).astype(f32)
    step = jnp.exp(log_step.astype(f32))[:, None]
    lr, li = lam_re.astype(f32), lam_im.astype(f32)
    decay = jnp.exp(lr * step)
    a_re, a_im = decay * jnp.cos(li * step), decay * jnp.sin(li * step)
    den = lr * lr + li * li
    f_re = ((a_re - 1.0) * lr + a_im * li) / den
    f_im = (a_im * lr - (a_re - 1.0) * li) / den
    br, bi = cmul(f_re[..., None], f_im[..., None], b_re.astype(f32), b_im.astype(f32))
    cr, ci = c_re.astype(f32), c_im.astype(f32)

    def combine(e_i, e_j):
        ar_i, ai_i, xr_i, xi_i = e_i
        ar_j, ai_j, xr_j, xi_j = e_j
        ar, ai = cmul(ar_j, ai_j, ar_i, ai_i)
        xr, xi = cmul(ar_j, ai_j, xr_i, xi_i)
        return ar, ai, xr + xr_j, xi + xi_j

    def scan_sequence(u_seq):
        bu_re = jnp.einsum('gnk,lgk->lgn', br, u_seq)
        bu_im = jnp.einsum('gnk,lgk->lgn', bi, u_seq)
        ar_seq = jnp.broadcast_to(a_re, bu_re.shape)
        ai_seq = jnp.broadcast_to(a_im, bu_im.shape)
        _, _, xr, xi = lax.associative_scan(combine, (ar_seq, ai_seq, bu_re, bu_im), axis=0)
        return jnp.einsum('gkn,lgn->lgk', cr, xr) - jnp.einsum('gkn,lgn->lgk', ci, xi)

    y = lax.map(scan_sequence, u)
    y = y + d_skip.astype(f32).reshape(SSM_GROUPS, SSM_GROUP) * u
    z = jax.nn.gelu(y.reshape(bsz, seq, D_MODEL)).astype(h.dtype)
    val, gate = jnp.split(z @ w_glu, 2, axis=-1)
    return val * jax.nn.sigmoid(gate)

def rope_tables(positions):
    inv_freq = ROPE_THETA ** (-jnp.arange(0, QK_ROPE_DIM, 2, dtype=jnp.float32) / QK_ROPE_DIM)
    ang = positions.astype(jnp.float32)[..., None] * inv_freq
    return jnp.cos(ang), jnp.sin(ang)

def apply_rope(x, cos, sin):
    x1, x2 = jnp.split(x.astype(jnp.float32), 2, axis=-1)
    return jnp.concatenate([x1 * cos - x2 * sin, x1 * sin + x2 * cos], axis=-1).astype(x.dtype)

def mla_shared_kv(h, w_kv_a, kv_a_norm, w_kv_b, k_nope_norm, k_rope_norm, cos, sin):
    bsz, seq, _ = h.shape
    ckv = h @ w_kv_a
    c_kv = rms_norm_2(ckv[..., :KV_LORA_RANK], kv_a_norm)
    k_rope = apply_rope(rms_norm_2(ckv[..., KV_LORA_RANK:], k_rope_norm), cos, sin)
    kv = (c_kv @ w_kv_b).reshape(bsz, seq, N_HEADS, QK_NOPE_DIM + V_DIM)
    k_nope = rms_norm_2(kv[..., :QK_NOPE_DIM], k_nope_norm)
    v = kv[..., QK_NOPE_DIM:]
    k_rope = jnp.broadcast_to(k_rope[:, :, None, :], (bsz, seq, N_HEADS, QK_ROPE_DIM))
    k = jnp.concatenate([k_nope, k_rope], axis=-1)
    return k.transpose(0, 2, 1, 3), v.transpose(0, 2, 1, 3)

def mla_queries(h, w_q_a, q_a_norm, w_q_b, q_nope_norm, q_rope_norm, cos, sin):
    bsz, seq, _ = h.shape
    c_q = rms_norm_2(h @ w_q_a, q_a_norm)
    q = (c_q @ w_q_b).reshape(bsz, seq, N_HEADS, QK_DIM)
    q_nope = rms_norm_2(q[..., :QK_NOPE_DIM], q_nope_norm)
    q_rope = apply_rope(rms_norm_2(q[..., QK_NOPE_DIM:], q_rope_norm),
                        cos[:, :, None, :], sin[:, :, None, :])
    return jnp.concatenate([q_nope, q_rope], axis=-1).transpose(0, 2, 1, 3)

def causal_block_attention(q, k, v):
    bsz, n_heads, seq, dk = q.shape
    dv = v.shape[-1]
    n_blocks = seq // Q_BLOCK
    q_blocks = q.reshape(bsz, n_heads, n_blocks, Q_BLOCK, dk).transpose(2, 0, 1, 3, 4)
    scale = 1.0 / math.sqrt(dk)
    key_pos = jnp.arange(seq)

    def one_block(args):
        q_blk, blk_idx = args
        s = jnp.einsum('bhqd,bhkd->bhqk', q_blk, k).astype(jnp.float32) * scale
        query_pos = blk_idx * Q_BLOCK + jnp.arange(Q_BLOCK)
        s = jnp.where(key_pos[None, :] <= query_pos[:, None], s, NEG_INF)
        p = jax.nn.softmax(s, axis=-1).astype(v.dtype)
        return jnp.einsum('bhqk,bhkd->bhqd', p, v)

    o = lax.map(one_block, (q_blocks, jnp.arange(n_blocks)))
    return o.transpose(1, 2, 0, 3, 4).reshape(bsz, n_heads, seq, dv)

def second_inputs(seed: int = 0) -> dict:
    key = jax.random.key(seed)
    ks = jax.random.split(key, 32)
    f32 = jnp.float32

    def dense(k, shape, fan_in):
        return jax.random.normal(k, shape, f32) * fan_in ** -0.5

    def gain(k, shape):
        return 1.0 + 0.02 * jax.random.normal(k, shape, f32)

    na, nb = N_A_LAYERS, N_B_LAYERS
    g, n, kk = SSM_GROUPS, SSM_STATE, SSM_GROUP
    x = jax.random.normal(ks[0], (BATCH, SEQ, D_MODEL), f32)
    positions = (jnp.arange(SEQ, dtype=jnp.int32)[None, :]
                 + jax.random.randint(ks[1], (BATCH, 1), 0, SEQ, dtype=jnp.int32))
    mix_norm = gain(ks[2], (DEPTH_2, D_MODEL))
    ffn_norm = gain(ks[3], (DEPTH_2, D_MODEL))
    ffn_w_gate_up = dense(ks[4], (DEPTH_2, D_MODEL, 2 * D_FF_2), D_MODEL)
    ffn_w_down = dense(ks[5], (DEPTH_2, D_FF_2, D_MODEL), D_FF_2)
    ssm_w_in = dense(ks[6], (na, D_MODEL, D_MODEL), D_MODEL)
    ssm_lambda_re = -0.5 + 0.01 * jax.random.normal(ks[7], (na, g, n), f32)
    ssm_lambda_im = (jnp.pi * jnp.arange(n, dtype=f32)
                     + 0.01 * jax.random.normal(ks[8], (na, g, n), f32))
    ssm_log_step = jax.random.uniform(ks[9], (na, g), f32,
                                      minval=math.log(STEP_MIN), maxval=math.log(STEP_MAX))
    ssm_b_re = dense(ks[10], (na, g, n, kk), 2 * kk)
    ssm_b_im = dense(ks[11], (na, g, n, kk), 2 * kk)
    ssm_c_re = dense(ks[12], (na, g, kk, n), 2 * n)
    ssm_c_im = dense(ks[13], (na, g, kk, n), 2 * n)
    ssm_d = jax.random.normal(ks[14], (na, D_MODEL), f32)
    ssm_w_glu = dense(ks[15], (na, D_MODEL, 2 * D_MODEL), D_MODEL)
    kv_in_norm = gain(ks[16], (D_MODEL,))
    mla_w_kv_a = dense(ks[17], (D_MODEL, KV_LORA_RANK + QK_ROPE_DIM), D_MODEL)
    mla_kv_a_norm = gain(ks[18], (KV_LORA_RANK,))
    mla_w_kv_b = dense(ks[19], (KV_LORA_RANK, N_HEADS * (QK_NOPE_DIM + V_DIM)), KV_LORA_RANK)
    mla_k_nope_norm = gain(ks[20], (QK_NOPE_DIM,))
    mla_k_rope_norm = gain(ks[21], (QK_ROPE_DIM,))
    mla_w_q_a = dense(ks[22], (nb, D_MODEL, Q_LORA_RANK), D_MODEL)
    mla_q_a_norm = gain(ks[23], (nb, Q_LORA_RANK))
    mla_w_q_b = dense(ks[24], (nb, Q_LORA_RANK, N_HEADS * QK_DIM), Q_LORA_RANK)
    mla_q_nope_norm = gain(ks[25], (nb, QK_NOPE_DIM))
    mla_q_rope_norm = gain(ks[26], (nb, QK_ROPE_DIM))
    mla_w_o = dense(ks[27], (nb, N_HEADS * V_DIM, D_MODEL), N_HEADS * V_DIM)
    return {
        'x': x, 'positions': positions,
        'mix_norm': mix_norm, 'ffn_norm': ffn_norm,
        'ffn_w_gate_up': ffn_w_gate_up, 'ffn_w_down': ffn_w_down,
        'ssm_w_in': ssm_w_in, 'ssm_lambda_re': ssm_lambda_re, 'ssm_lambda_im': ssm_lambda_im,
        'ssm_log_step': ssm_log_step, 'ssm_b_re': ssm_b_re, 'ssm_b_im': ssm_b_im,
        'ssm_c_re': ssm_c_re, 'ssm_c_im': ssm_c_im, 'ssm_d': ssm_d, 'ssm_w_glu': ssm_w_glu,
        'kv_in_norm': kv_in_norm, 'mla_w_kv_a': mla_w_kv_a, 'mla_kv_a_norm': mla_kv_a_norm,
        'mla_w_kv_b': mla_w_kv_b, 'mla_k_nope_norm': mla_k_nope_norm,
        'mla_k_rope_norm': mla_k_rope_norm,
        'mla_w_q_a': mla_w_q_a, 'mla_q_a_norm': mla_q_a_norm, 'mla_w_q_b': mla_w_q_b,
        'mla_q_nope_norm': mla_q_nope_norm, 'mla_q_rope_norm': mla_q_rope_norm,
        'mla_w_o': mla_w_o,
    }

def second_block(x, positions, mix_norm, ffn_norm, ffn_w_gate_up, ffn_w_down,
              ssm_w_in, ssm_lambda_re, ssm_lambda_im, ssm_log_step, ssm_b_re, ssm_b_im,
              ssm_c_re, ssm_c_im, ssm_d, ssm_w_glu,
              kv_in_norm, mla_w_kv_a, mla_kv_a_norm, mla_w_kv_b, mla_k_nope_norm,
              mla_k_rope_norm, mla_w_q_a, mla_q_a_norm, mla_w_q_b, mla_q_nope_norm,
              mla_q_rope_norm, mla_w_o):
    bsz, seq, _ = x.shape
    cos, sin = rope_tables(positions)
    k_shared, v_shared = None, None
    for layer in range(DEPTH_2):
        h = rms_norm_2(x, mix_norm[layer])
        if layer < N_A_LAYERS:
            i = layer
            x = x + s5_mixer(h, ssm_w_in[i], ssm_lambda_re[i], ssm_lambda_im[i], ssm_log_step[i],
                             ssm_b_re[i], ssm_b_im[i], ssm_c_re[i], ssm_c_im[i], ssm_d[i],
                             ssm_w_glu[i])
        else:
            j = layer - N_A_LAYERS
            if j == 0:
                k_shared, v_shared = mla_shared_kv(rms_norm_2(x, kv_in_norm), mla_w_kv_a,
                                                   mla_kv_a_norm, mla_w_kv_b, mla_k_nope_norm,
                                                   mla_k_rope_norm, cos, sin)
            q = mla_queries(h, mla_w_q_a[j], mla_q_a_norm[j], mla_w_q_b[j],
                            mla_q_nope_norm[j], mla_q_rope_norm[j], cos, sin)
            o = causal_block_attention(q, k_shared, v_shared)
            o = o.transpose(0, 2, 1, 3).reshape(bsz, seq, N_HEADS * V_DIM)
            x = x + o @ mla_w_o[j]
        x = x + swiglu_ffn(rms_norm_2(x, ffn_norm[layer]), ffn_w_gate_up[layer], ffn_w_down[layer])
    return x


def setup_inputs(seed=0):
    out = dict(first_inputs(seed))
    for name, value in second_inputs(seed + 1).items():
        if name != "x":
            out[name + "_2"] = value
    return out


def reference(
    x, norm_mix_pre, w_in, conv_qkv_w, gdn_a_log, gdn_dt_bias, gdn_norm_w, conv_sc_w, w_branch,
    w_out, norm_mix_post, norm_ffn_pre, w_ff1, w_ff2, norm_ffn_post, positions_2, mix_norm_2,
    ffn_norm_2, ffn_w_gate_up_2, ffn_w_down_2, ssm_w_in_2, ssm_lambda_re_2, ssm_lambda_im_2,
    ssm_log_step_2, ssm_b_re_2, ssm_b_im_2, ssm_c_re_2, ssm_c_im_2, ssm_d_2, ssm_w_glu_2,
    kv_in_norm_2, mla_w_kv_a_2, mla_kv_a_norm_2, mla_w_kv_b_2, mla_k_nope_norm_2,
    mla_k_rope_norm_2, mla_w_q_a_2, mla_q_a_norm_2, mla_w_q_b_2, mla_q_nope_norm_2,
    mla_q_rope_norm_2, mla_w_o_2,
):
    x = first_block(
        x, norm_mix_pre, w_in, conv_qkv_w, gdn_a_log, gdn_dt_bias, gdn_norm_w, conv_sc_w,
        w_branch, w_out, norm_mix_post, norm_ffn_pre, w_ff1, w_ff2, norm_ffn_post,
    )
    return second_block(
        x, positions_2, mix_norm_2, ffn_norm_2, ffn_w_gate_up_2, ffn_w_down_2, ssm_w_in_2,
        ssm_lambda_re_2, ssm_lambda_im_2, ssm_log_step_2, ssm_b_re_2, ssm_b_im_2, ssm_c_re_2,
        ssm_c_im_2, ssm_d_2, ssm_w_glu_2, kv_in_norm_2, mla_w_kv_a_2, mla_kv_a_norm_2,
        mla_w_kv_b_2, mla_k_nope_norm_2, mla_k_rope_norm_2, mla_w_q_a_2, mla_q_a_norm_2,
        mla_w_q_b_2, mla_q_nope_norm_2, mla_q_rope_norm_2, mla_w_o_2,
    )


_drawn_inputs = setup_inputs


def setup_inputs(seed=0):
    import zlib

    import numpy as np

    out = dict(_drawn_inputs(seed))
    spreads = {}
    factors = {'gdn_norm_w': 7.394,
     'norm_mix_post': 3.52,
     'norm_ffn_pre': 3.852,
     'norm_ffn_post': 4.439,
     'mix_norm_2': 8.0,
     'ffn_norm_2': 4.333,
     'ssm_lambda_re_2': 64.0,
     'ssm_lambda_im_2': 32.416,
     'ssm_log_step_2': 20.327,
     'ssm_b_re_2': 31.357,
     'ssm_b_im_2': 34.733,
     'ssm_c_re_2': 34.672,
     'ssm_c_im_2': 40.939,
     'kv_in_norm_2': 8.0,
     'mla_kv_a_norm_2': 8.0,
     'mla_k_nope_norm_2': 8.0,
     'mla_k_rope_norm_2': 8.0,
     'mla_q_a_norm_2': 8.0,
     'mla_q_nope_norm_2': 8.0,
     'mla_q_rope_norm_2': 8.0}
    for name, (base, spread) in spreads.items():
        noise = np.random.default_rng([zlib.crc32(name.encode()), seed]).standard_normal(out[name].shape)
        drawn = base * np.exp(spread * noise) if base else spread * noise
        out[name] = jnp.asarray(drawn.astype(out[name].dtype))
    for name, factor in factors.items():
        out[name] = (out[name] * factor).astype(out[name].dtype)
    return out
```

```python
from contextlib import ExitStack

import concourse.bass as bass
from concourse import mybir

F32 = mybir.dt.float32
F32R = mybir.dt.float32r
I32 = mybir.dt.int32
ACT = mybir.ActivationFunctionType
ALU = mybir.AluOpType
AX_X = mybir.AxisListType.X

P = 128
SEQ = 512
D = 1024
KD = D // P
EPS = 1e-6
CREDIT = 2
NEG = -1e30
LN_EXP = "natural_log_exp_and_others"

GH = 4
CHUNK = 128
NCH = SEQ // CHUNK
LEVELS = 7
SB_PAIRS = 4
FF1_HALF = 16
FF1_UNITS = 2
F2T = 22
GROUPS, GCH, NST = 64, 16, 64
SUB = 8
NSUB = SEQ // SUB
NQ = GROUPS // 2
QB = 8
MH = 16
QK = 96
TWO_PI = 6.283185307179586
PI_BELOW = 3.1415925
PREP = 4
MAGIC = 12582912.0
C1, C2, C3 = 6.28125, 0.0019350051879882812, 3.019916e-07

STREAM = [
    ("ab", 1, [8]), ("qkv", 12, [8]), ("gate", 4, [8]), ("sb", 12, [8]), ("sc", 12, [8]),
    ("merge", 32, [8, 8, 8, 12]), ("wout", 8, [8]),
    ("up_a", 16, [8]), ("down_a", 16, [8]), ("up_b", 16, [8]), ("down_b", 16, [8]),
    ("ssm_in", 8, [8]), ("glu", 16, [8]), ("gu0", 44, [8]), ("dn0", 16, [11]),
    ("qa", 3, [8]), ("qb", 4, [12]), ("kva", 3, [8]), ("kvb", 4, [8]),
    ("wo", 8, [8]), ("gu1", 44, [8]), ("dn1", 16, [11]),
]
KTS, U0 = [], {}
for _name, _n, _period in STREAM:
    U0[_name] = len(KTS)
    KTS += [_period[i % len(_period)] for i in range(_n)]
NU = len(KTS)

PCOL, _at = {}, 0
for _name, _n in [("mix_pre", 8), ("mix_post", 8), ("ffn_pre", 8), ("ffn_post", 8), ("conv_qkv", 48), ("conv_sc", 12),
                  ("gdn_norm", 1), ("a_log", 1), ("dt_bias", 1), ("mix0", 8), ("mix1", 8), ("ffn0", 8), ("ffn1", 8),
                  ("kv_in", 8), ("d_skip", 8), ("kv_a", 2), ("q_a", 3), ("k_head", 1), ("q_head", 1),
                  ("inv_freq", 1), ("eps", 1)]:
    PCOL[_name] = _at
    _at += _n
NPAR = _at

CONST = ["ident", "ones", "incl", "strict", "lev0", "lev1", "lev2", "lev3", "lev4", "lev5", "lev6",
         "sel0", "sel1", "sel2", "sel3", "sel4", "sel5", "sel6", "sel7",
         "negtri", "negones", "sbmask", "shift0", "shift1", "shift2", "shift3", "shift4", "shift5", "shift6", "shift7",
         "blk96", "rot", "mlamask"]
CIX = {n: i for i, n in enumerate(CONST)}


def unit_loop(eng, n, period, body, chain=None, ops=0, look=0, u0=0):
    trips = (n - look) // period
    if trips > 1:
        for i in range(trips * period):
            assert KTS[u0 + i + look] == KTS[u0 + i % period + look]
        with eng.Fori(0, trips) as j:
            start = chain.n if chain else 0
            if chain:
                chain.off = j * ops
            for s in range(period):
                body(s, j)
            if chain:
                assert chain.n - start == ops, (chain.n - start, ops)
                chain.off, chain.n = 0, start + ops * trips
    else:
        trips = 0
    for i in range(trips * period, n):
        body(i, 0)


class Chain:

    def __init__(self, eng, sem):
        self.eng, self.sem, self.n, self.off = eng, sem, 0, 0

    def __call__(self, ins):
        ins.then_inc(self.sem, 1)
        self.n += 1
        self.eng.wait_ge(self.sem, self.off + self.n)


def build(nc, t_x, t_par, t_const, t_w, t_pos, t_ssm, t_out, t_scratch_u, t_scratch_y):
    ctx = ExitStack()
    with ctx:
        def sem(name):
            return ctx.enter_context(nc.semaphore(name))

        base = [16512]

        def fixed(name, shape, dt=F32):
            size = 4
            for n in shape[1:]:
                size *= n
            t = nc.alloc_sbuf_tensor_at(name, shape, dt, offset=base[0])
            base[0] += (size + 31) // 32 * 32
            return t

        x = fixed("x", [P, KD, SEQ])
        h_hi, h_lo = fixed("h_hi", [P, KD, SEQ], F32R), fixed("h_lo", [P, KD, SEQ], F32R)
        scan_tmp = nc.alloc_sbuf_tensor_at("scan_tmp", [P, 2, 2048], F32, offset=base[0] - 32768)
        pow_tmp = nc.alloc_sbuf_tensor_at("pow_tmp", [P, 2, QB * SUB * GCH], F32, offset=base[0] - 16384)
        w_raw = fixed("w_raw", [P, 2, 12, P])
        w_hi, w_lo = fixed("w_hi", [P, 2, 12, P], F32R), fixed("w_lo", [P, 2, 12, P], F32R)
        TOEP1 = base[0]
        stage, val, sq = fixed("stage", [P, 2, SEQ]), fixed("val", [P, 2, SEQ]), fixed("sq", [P, 2, SEQ])
        rs = fixed("rs", [P, SEQ])
        ident, ones = fixed("ident", [P, P]), fixed("ones", [P, P])
        par = fixed("par", [P, NPAR])
        ARENA = base[0]
        assert ARENA + 110112 <= 229368, ARENA

        def at(name, off, shape, dt=F32):
            size = 4
            for n in shape[1:]:
                size *= n
            assert off + size <= 110112 and off % 32 == 0, (name, off + size)
            return nc.alloc_sbuf_tensor_at(name, shape, dt, offset=ARENA + off)

        y_hi = [at(f"y{b}_hi", 16384 * b, [P, 4, SEQ], F32R) for b in range(3)]
        y_lo = [at(f"y{b}_lo", 16384 * b + 8192, [P, 4, SEQ], F32R) for b in range(3)]
        Gb, Bb = at("Gb", 0, [P, GH, SEQ]), at("Bb", 8192, [P, GH, SEQ])
        Tm, Um = at("Tm", 0, [P, NCH, GH, P]), at("Um", 8192, [P, NCH, GH, P])
        qkv = at("qkv", 16384, [P, 12, SEQ])
        o_t = at("o_t", 16384, [P, GH, SEQ])
        Xm = at("Xm", 24576, [P, NCH, GH, P])
        vnew = at("vnew", 24576, [P, 2, GH, P])
        AM = at("AM", 32768, [P, NCH, GH, P])
        gsil = at("gsil", 40960, [P, GH, SEQ])
        qd = at("qd", 49152, [P, GH, SEQ])
        g_rows, b_rows = at("g_rows", 49152, [8, SEQ]), at("b_rows", 51200, [8, SEQ])
        cbuf = at("cbuf", 57344, [P, 2, 3 + SEQ])
        akk, aqk = at("akk", 57344, [P, NCH, GH, P]), at("aqk", 65536, [P, NCH, GH, P])
        kbg, kdec, vb = (at(n, 73728 + 8192 * i, [P, NCH, GH, P]) for i, n in enumerate(("kbg", "kdec", "vb")))
        gc = at("gc", 98304, [P, 17, P])
        S = at("S", 107008, [P, GH, P])
        gcol, bcol = at("gcol", 109056, [P, NCH, 8]), at("bcol", 109184, [P, NCH, 8])
        egc, kdc, glc = (at(n, 109312 + 64 * i, [P, NCH, GH]) for i, n in enumerate(("egc", "kdc", "glc")))
        sbq, sbk = at("sbq", 32768, [P, 2, SEQ]), at("sbk", 36864, [P, 2, SEQ])
        vpad = at("vpad", 40960, [P, 2, 4, 2, P])
        Lb, att, ez = at("Lb", 49152, [P, 4, SEQ]), at("att", 57344, [P, 4, SEQ]), at("ez", 65536, [P, 4, SEQ])
        sbc = at("sbc", 73728, [P, 3, P])
        scc = at("scc", 49152, [P, 2, SEQ])
        scx = at("scx", 53248, [P, 2, 2 + SEQ])
        sct = at("sct", 57376, [P, 2, SEQ])
        m_hi, m_lo = at("m_hi", 49152, [P, KD, SEQ], F32R), at("m_lo", 65536, [P, KD, SEQ], F32R)
        gsig, mt = at("gsig", 81920, [P, 3, SEQ]), at("mt", 94208, [P, 2, SEQ])
        y = at("y", 0, [P, KD, SEQ])
        f_hi, f_lo = at("f_hi", 0, [P, 16, SEQ], F32R), at("f_lo", 32768, [P, 16, SEQ], F32R)
        ysum = at("ysum", 65536, [P, KD, SEQ])
        relu = at("relu", 81920, [P, 2, SEQ])
        e_hi, e_lo = at("e_hi", 0, [P, F2T, SEQ], F32R), at("e_lo", 45056, [P, F2T, SEQ], F32R)
        sgate = at("sgate", 90112, [P, 2, SEQ])

        u_t, u_b = at("u_t", 0, [P, KD, SEQ]), at("u_b", 16384, [P, GROUPS, NSUB])
        xp = at("xp", 32768, [P, NSUB, 2, NQ])
        y_t = at("y_t", 32768, [P, KD, SEQ])
        b_pow, l_in = at("b_pow", 49152, [P, QB, 2, P]), at("l_in", 57344, [P, QB, 2, P])
        toep, c_pow = at("toep", 65536, [P, 2 * QB, SUB, GCH]), at("c_pow", 73728, [P, QB, 2, P])
        k_lag = at("k_lag", 81920, [P, GROUPS * GCH])
        pw = at("pw", 86016, [P, 2, SUB + 1, NQ])
        spar = at("spar", 88576, [P, 3 * NQ + 4 * NQ * GCH])
        sm = at("sm", 97152, [P, 12, NQ])
        bbar = at("bbar", 98688, [P, 2, NQ, GCH])
        shifts = at("shifts", 102784, [P, SUB, P])
        pa = at("pa", 106880, [P, 2, 8, NQ])
        b_pows = [b_pow, at("b_pow1", 73728, [P, QB, 2, P])]
        c_pows = [at("c_pow0", 49152, [P, QB, 2, P]), c_pow, at("c_pow2", 57344, [P, QB, 2, P])]
        toeps = [toep, nc.alloc_sbuf_tensor_at("toep1", [P, 2 * QB, SUB, GCH], F32, offset=TOEP1)]
        sgl = at("sgl", 49152, [P, 2, SEQ])
        cq_raw = at("cq_raw", 0, [P, 3, SEQ])
        cq_hi, cq_lo = at("cq_hi", 6144, [P, 3, SEQ], F32R), at("cq_lo", 12288, [P, 3, SEQ], F32R)
        ck_hi, ck_lo = at("ck_hi", 0, [P, 2, SEQ], F32R), at("ck_lo", 4096, [P, 2, SEQ], F32R)
        v_t = at("v_t", 8192, [P, 4, MH, 64])
        ck_raw, kr_raw = at("ck_raw", 24576, [P, 2, SEQ]), at("kr_raw", 28672, [P, SEQ])
        rs_keep = at("rs_keep", 30720, [P, SEQ])
        kh, qh = at("kh", 32768, [P, MH, SEQ]), at("qh", 65536, [P, MH, SEQ])
        cos_t, sin_t = at("cos_t", 98304, [P, SEQ]), at("sin_t", 100352, [P, SEQ])
        mlac = at("mlac", 102400, [P, 3, P])
        nmax, psums = at("nmax", 103936, [P, 2, 4]), at("psums", 103968, [P, 2, 4])
        pos_i = at("pos_i", 104000, [P, SEQ], I32)
        ang = at("ang", 106048, [P, SEQ])
        p_bs, p_t = [at("p_b0", 0, [P, 1280]), at("p_b1", 104000, [P, 1280])], at("p_t", 24576, [P, 4, SEQ])

        ps = ctx.enter_context(nc.psum_tensor("ps", [P, 8, SEQ], F32))

        params_in, x_in, consts_in, sbc_in = sem("params_in"), sem("x_in"), sem("consts_in"), sem("sbc_in")
        raw_in = [sem("raw_in0"), sem("raw_in1")]
        hi_done, lo_done, w_used = sem("hi_done"), sem("lo_done"), sem("w_used")
        acc_done, acc_free = sem("acc_done"), sem("acc_free")
        stage_full, stage_free = sem("stage_full"), sem("stage_free")
        val_full, val_hi, val_lo = sem("val_full"), sem("val_hi"), sem("val_lo")
        sq_full, sq_used, root_done = sem("sq_full"), sem("sq_used"), sem("root_done")
        act_chain, dve_chain, pool_chain = sem("act_chain"), sem("dve_chain"), sem("pool_chain")
        x_ready, part_done, vpad_zero = sem("x_ready"), sem("part_done"), sem("vpad_zero")
        ab_abs, ab_exp, ab_sig, g_ready = sem("ab_abs"), sem("ab_exp"), sem("ab_sig"), sem("g_ready")
        l2_root, l2_done, bc_done, bc_copied = sem("l2_root"), sem("l2_done"), sem("bc_done"), sem("bc_copied")
        cols_done, kdc_sub, cols_exp, qd_exp = sem("cols_done"), sem("kdc_sub"), sem("cols_exp"), sem("qd_exp")
        tok_done, tok_used, kq_done, akk_done = sem("tok_done"), sem("tok_used"), sem("kq_done"), sem("akk_done")
        dmin_done, dec_done = sem("dmin_done"), sem("dec_done")
        am_done, x_done, xs_done, dtu_done, tu_done = (
            sem("am_done"), sem("x_done"), sem("xs_done"), sem("dtu_done"), sem("tu_done"))
        uw_done, u_copied, w_copied = sem("uw_done"), sem("u_copied"), sem("w_copied")
        ws_done, vn_done, o_done, o_copied = sem("ws_done"), sem("vn_done"), sem("o_done"), sem("o_copied")
        ds_done, s_done = sem("ds_done"), sem("s_done")
        sb_z, sb_ln, sb_l = sem("sb_z"), sem("sb_ln"), sem("sb_l")
        sb_suf, sb_att, sb_o = sem("sb_suf"), sem("sb_att"), sem("sb_o")
        prep_act, prep_dve, spar_in, zeros_done = sem("prep_act"), sem("prep_dve"), sem("spar_in"), sem("zeros_done")
        u_out, u_in, y_out, y_in = sem("u_out"), sem("u_in"), sem("y_out"), sem("y_in")
        bp_done = [sem("bp_done_dve"), sem("bp_done_pool")]
        lt_done, lin_done, kl_done, kl_copied = (
            sem("lt_done"), sem("lin_done"), sem("kl_done"), sem("kl_copied"))
        xi_done, xi_copied, scan_done = sem("xi_done"), sem("xi_copied"), sem("scan_done")
        cp_done, tp_done, tp_copied, y_done, y_copied = (
            sem("cp_done"), sem("tp_done"), sem("tp_copied"), sem("y_done"), sem("y_copied"))
        z_sum, rope_in, trig_arg, trig_done = sem("z_sum"), sem("rope_in"), sem("trig_arg"), sem("trig_done")
        kr_copied, hn_sum, hn_root, hn_scaled, hn_rot, hn_done = (
            sem("kr_copied"), sem("hn_sum"), sem("hn_root"), sem("hn_scaled"), sem("hn_rot"), sem("hn_done"))
        hn_sq = sem("hn_sq")
        at_q, at_s, at_max, at_p, at_pt, at_ptc, at_ptd, at_o, at_oc, at_ot = (
            sem("at_q"), sem("at_s"), sem("at_max"), sem("at_p"), sem("at_pt"), sem("at_ptc"), sem("at_ptd"),
            sem("at_o"), sem("at_oc"), sem("at_ot"))
        out_done, gc_in = sem("out_done"), sem("gc_in")

        T0, V0, G0, VF, n_t, n_v, n_g, n_f = {}, {}, {}, {}, 0, 0, 0, 0
        for name, nt, nv, ng in [
            ("h_mix", 0, 8, 0), ("ab", 1, 0, 0), ("qkv", 12, 0, 12), ("gate", 4, 0, 4), ("gdn", 0, 4, 0),
            ("sb", 12, 4, 0), ("sc", 12, 4, 0), ("merge", 48, 8, 24), ("wout", 8, 0, 0), ("h_ffn", 0, 8, 0),
            ("up_a", 16, 16, 0), ("down_a", 8, 0, 0), ("up_b", 16, 16, 0), ("down_b", 8, 0, 0),
            ("h_mix0", 0, 8, 0), ("ssm_in", 8, 0, 0), ("z", 0, 8, 8), ("glu", 16, 0, 8), ("h_ffn0", 0, 8, 0),
            ("gu0", 44, 22, 22), ("dn0", 8, 0, 0), ("h_mix1", 0, 8, 0), ("qa", 3, 3, 0), ("qb", 16, 0, 0),
            ("h_kv", 0, 8, 0), ("kva", 3, 2, 0), ("kvb", 24, 0, 0), ("attn", 0, 8, 0), ("wo", 8, 0, 0),
            ("h_ffn1", 0, 8, 0), ("gu1", 44, 22, 22), ("dn1", 8, 0, 0),
        ]:
            T0[name], V0[name], G0[name], VF[name] = n_t, n_v, n_g, n_f
            n_t, n_v, n_g = n_t + nt, n_v + nv, n_g + ng
            n_f += nv if name in ("gu0", "gu1", "z", "attn") else 0

        def pc(name, i=0, rows=slice(0, P)):
            c = PCOL[name]
            if isinstance(i, int):
                return par[rows, c + i:c + i + 1]
            return par[rows, bass.ds(i + c, 1)]

        def one(t, i):
            if isinstance(i, int):
                return t[:, i, :]
            return t[:, bass.ds(i, 1), :].rearrange("p a n -> p (a n)")

        g_last = Gb[:, :, :].rearrange("p h (c n) -> p c h n", n=CHUNK)[:, :, :, CHUNK - 1]

        mt_f = at("turns", 24576, [P, SEQ])

        def c_par(comp, rows, q):
            c = 3 * NQ + (2 + comp) * NQ * GCH + q * GCH
            return spar[rows, c:c + GCH]

        def p_block(a, tb):
            o = P * tb * (tb + 1) // 2
            return p_bs[a % 2][:, o:o + P * tb + P]

        def s_block(a, tb):
            bank, col = ((1, 3 * P), (2, 0), (1, 0), (0, 0))[tb]
            return ps[:, 3 * (a % 2) + bank, col:col + P * tb + P]

        def o_block(a, tb):
            return ps[:, 3 * (a % 2) + 2, 256 + 64 * tb:320 + 64 * tb]

        def t_unit(i, j=0):
            n = 4 * i + i // 2
            return j * 18 + n, n

        def head_steps(eng, body, chain=None, ops=0):
            for h in range(3):
                body(h, 0)
            with eng.Fori(0, 6) as j:
                n0 = chain.n if chain else 0
                if chain:
                    chain.off = j * ops
                body(3, j)
                body(4, j)
                if chain:
                    assert chain.n - n0 == ops
                    chain.off, chain.n = 0, n0 + 6 * ops
            body(MH - 1, 0)

        def over_heads(eng, body, chain=None, ops=0):
            body(0, 0)
            body(1, 0)
            with eng.Fori(0, 3) as j:
                n0 = chain.n if chain else 0
                if chain:
                    chain.off = j * ops
                for i in range(2, 6):
                    body(i, j)
                if chain:
                    assert chain.n - n0 == ops
                    chain.off, chain.n = 0, n0 + 3 * ops
            body(14, 0)
            body(15, 0)

        def powers(eng, link, tmp, dst, b, first, v_re, v_im, minus):
            qs = slice(QB * b, QB * b + QB)
            for comp in range(2):
                for n, (w, v) in enumerate(((0, (v_re, v_im)[comp]), (1, (v_im, v_re)[comp]))):
                    m = pw[:, w, first:first + SUB, qs].rearrange("p i q -> p q i").unsqueeze(3)\
                        .to_broadcast([P, QB, SUB, GCH])
                    v_b = v[:, qs, :].unsqueeze(2).to_broadcast([P, QB, SUB, GCH])
                    ins = eng.tensor_tensor(tmp[n], m, v_b, ALU.mult)
                    if n:
                        link(ins)
                ins = eng.tensor_tensor(dst[:, :, comp, :].rearrange("p q (i k) -> p q i k", k=GCH),
                                        tmp[0], tmp[1], (ALU.subtract, ALU.add)[comp != minus])
                if comp == 0:
                    link(ins)
            return ins

        def par_b(n):
            return spar[:, 3 * NQ + n * NQ * GCH:3 * NQ + (n + 1) * NQ * GCH].rearrange("p (q k) -> p q k", k=GCH)

        block = ctx.enter_context(nc.Block())

        @block.sync
        def _(sp):
            sp.dma_start(par[:, :], t_par).then_inc(params_in, 16)
            sp.dma_start(x[:, :, :], t_x).then_inc(x_in, 16)
            sp.dma_start(ident[:, :], t_const[:, 0:P]).then_inc(consts_in, 16)
            sp.dma_start(ones[:, :], t_const[:, P:2 * P]).then_inc(consts_in, 16)
            sp.dma_start(gc[:, :, :].rearrange("p n c -> p (n c)"), t_const[:, 2 * P:19 * P]).then_inc(gc_in, 16)
            for phase, n, period in STREAM:
                u0 = U0[phase]

                per = max(2, len(period))

                def load(s, j):
                    k, slot, u = KTS[u0 + s], (u0 + s) % 2, j * per + (u0 + s)
                    unit = t_w[u] if isinstance(u, int) else t_w[bass.ds(u, 1)].rearrange("a p n -> (a p) n")
                    sp.wait_ge(lo_done, u + 1)
                    sp.dma_start(w_raw[:, slot, 0:k, :].rearrange("p k n -> p (k n)"), unit[:, 0:k * P])\
                      .then_inc(raw_in[slot], 16)

                unit_loop(sp, n, per, load, u0=u0)
                if phase == "ssm_in":
                    for k in range(KD):
                        sp.wait_ge(acc_free, T0["ssm_in"] + k + 1 + CREDIT)
                        sp.dma_start(t_scratch_u[k * P:(k + 1) * P].rearrange("d j c -> d (j c)"), u_t[:, k, :])\
                           .then_inc(u_out, 16)
                    sp.wait_ge(u_out, 16 * KD)
                    for r in range(SUB):
                        sp.dma_start(u_b[GCH * r:GCH * r + GCH, :, :],
                                      t_scratch_u.rearrange("(g k) j c -> j k g c", k=GCH)[SUB - 1 - r]).then_inc(u_in, 16)
            for half in range(2):
                sp.wait_ge(acc_free, T0["dn1"] + 4 * half + 4 + CREDIT)
                sp.dma_start(t_out[:, 4 * half:4 * half + 4, :], x[:, 4 * half:4 * half + 4, :]).then_inc(out_done, 16)
            sp.wait_ge(out_done, 32)
        def u_done(u):
            return w_used, u + 1 + CREDIT

        def cs(c):
            return slice(c * CHUNK, (c + 1) * CHUNK)

        @block.tensor
        def _(pe):
            stat = [0]

            def tile(u, s_u, k_n, out, xs, k0=0, w0=0, first=True, last=True, v=None, m=P):
                slot = s_u % 2
                for k in range(k_n):
                    if v is not None:
                        pe.wait_ge(val_lo, v + k0 + k + 1 + CREDIT)
                    for n, (w, o) in enumerate(((w_hi, xs[0]), (w_hi, xs[1]), (w_lo, xs[0]))):
                        mm = pe.matmul(out, w[:, slot, w0 + k, 0:m], o[:, k0 + k, :],
                                       start=first and k == 0 and n == 0, stop=last and k == k_n - 1 and n == 2)
                return mm

            def split_ready(u):
                pe.wait_ge(lo_done, u + 1 + CREDIT)

            def bank_free(t):
                pe.wait_ge(acc_free, t + 1)

            H = (h_hi, h_lo)

            def plain(phase, n, xs=H, v=None, k_units=1, sums=0):
                u0, t0 = U0[phase], T0[phase]
                deep = k_units * max(sums, 1)
                per, sq0 = 2 * deep, stat[0]

                def add_squares(g, j):
                    pe.wait_ge(sq_full, j * 2 + (sq0 + g + 1))
                    pe.matmul(ps[:, 7, :], ones[:, :], sq[:, (sq0 + g) % 2, :], start=at_start[0], stop=False,
                              skip_group_check=True).then_inc(sq_used, 1)
                    at_start[0] = False

                def body(s, j):
                    s = s + skip
                    q, m = s % k_units, s // k_units
                    u, t = j * per + (u0 + s), j * (per // k_units) + (t0 + m)
                    k_n = KTS[u0 + s]
                    split_ready(u)
                    if q == 0:
                        bank_free(t)
                    mm = tile(u, u0 + s, k_n, ps[:, (t0 + m) % 2, :], xs, k0=q * k_n, first=q == 0,
                              last=q == k_units - 1, v=v if first_tile[0] else None)
                    mm.then_inc(w_used, 1)
                    if sums and s % deep == deep - 1 and s >= deep:
                        add_squares(s // deep - 1, j)

                first_tile, at_start = [v is not None], [True]
                skip = 0
                if v is not None or sums:
                    for s in range(min(per, n * k_units)):
                        body(s, 0)
                        first_tile[0] = v is not None and s + 1 < k_units
                    skip = per
                if n * k_units > skip:
                    unit_loop(pe, n * k_units - skip, per, body, u0=u0 + skip)
                if sums:
                    add_squares(n // sums - 1, 0)
                    stat[0] += n // sums

            def stats(n=KD, bank=7, rows=P):
                for k in range(n):
                    pe.wait_ge(sq_full, stat[0] + 1)
                    pe.matmul(ps[:, bank, :], ones[:, :], sq[:, stat[0] % 2, :], start=k == 0, stop=k == n - 1)\
                      .then_inc(sq_used, 1)
                    stat[0] += 1

            def delta_rule():
                for j in range(2 * GH):
                    if j >= 2:
                        pe.wait_ge(l2_root, j - 1)
                    stats(1, bank=2 + j % 2)
                pe.wait_ge(gc_in, 16)
                pe.wait_ge(g_ready, 1)
                pe.wait_ge(ab_sig, 1)
                for m in range(2 * GH):
                    if m >= 2:
                        pe.wait_ge(bc_copied, m - 1)
                    rows = b_rows if m % 2 else g_rows
                    pe.matmul(ps[:, 4 + m % 2, :], gc[0:8, 9 + m // 2 + GH * (m % 2), :], rows[:, :],
                              start=True, stop=True).then_inc(bc_done, 1)
                for c in range(NCH):
                    pe.transpose(ps[:, 6, 8 * c:8 * c + 8], g_rows[:, cs(c)], ident[0:8, 0:8])
                    tr = pe.transpose(ps[:, 6, 32 + 8 * c:40 + 8 * c], b_rows[:, cs(c)], ident[0:8, 0:8])
                tr.then_inc(cols_done, 1)
                pe.wait_ge(l2_done, 2 * GH)
                pe.wait_ge(bc_copied, 2 * GH)
                for c in range(NCH):
                    if c:
                        pe.wait_ge(tok_used, c)
                    for h in range(GH):
                        pe.transpose(ps[:, 2, cs(h)], qkv[:, GH + h, cs(c)], ident[:, :])
                    for h in range(GH):
                        tr = pe.transpose(ps[:, 3, cs(h)], qkv[:, 2 * GH + h, cs(c)], ident[:, :])
                    tr.then_inc(tok_done, 1)
                    if c:
                        pe.wait_ge(akk_done, c)
                    for h in range(GH):
                        k_c = qkv[:, GH + h, cs(c)]
                        pe.matmul(ps[:, 4, cs(h)], k_c, k_c, start=True, stop=True)
                    for h in range(GH):
                        mm = pe.matmul(ps[:, 5, cs(h)], qkv[:, GH + h, cs(c)], qkv[:, h, cs(c)], start=True, stop=True)
                    mm.then_inc(kq_done, 1)

                def update(n):
                    c = n % NCH
                    pe.wait_ge(xs_done, n + 1)
                    if n >= 2:
                        pe.wait_ge(tu_done, n - 1)
                    b = 4 + 2 * (n % 2)
                    if n < NCH * (LEVELS - 1):
                        for h in range(GH):
                            pe.matmul(ps[:, b, cs(h)], Um[:, c, h, :], Xm[:, c, h, :], start=True, stop=True)
                    for h in range(GH):
                        mm = pe.matmul(ps[:, b + 1, cs(h)], Xm[:, c, h, :], Um[:, c, h, :], start=True, stop=True)
                    mm.then_inc(dtu_done, 1)

                for n in range(NCH * LEVELS):
                    c = n % NCH
                    pe.wait_ge(am_done, n + 1)
                    if n >= NCH:
                        pe.wait_ge(tu_done, n - NCH + 1)
                    if n >= 2:
                        pe.wait_ge(xs_done, n - 1)
                    for h in range(GH):
                        mm = pe.matmul(ps[:, 2 + n % 2, cs(h)], AM[:, c, h, :], Tm[:, c, h, :], start=True, stop=True)
                    mm.then_inc(x_done, 1)
                    if n:
                        update(n - 1)
                update(NCH * LEVELS - 1)
                for c in range(NCH):
                    pe.wait_ge(tu_done, NCH * (LEVELS - 1) + c + 1)
                    if c >= 2:
                        pe.wait_ge(u_copied, c - 1)
                        pe.wait_ge(w_copied, c - 1)
                    if c == 1:
                        pe.wait_ge(tu_done, NCH * LEVELS)
                    b = 2 + 2 * (c % 2)
                    for h in range(GH):
                        pe.matmul(ps[:, b, cs(h)], Um[:, c, h, :], vb[:, c, h, :], start=True, stop=True)
                    for h in range(GH):
                        mm = pe.matmul(ps[:, b + 1, cs(h)], kbg[:, c, h, :], Um[:, c, h, :], start=True, stop=True)
                    mm.then_inc(uw_done, 1)
                pe.wait_ge(u_copied, NCH)
                pe.wait_ge(w_copied, NCH)
                for c in range(NCH):
                    if c:
                        pe.wait_ge(s_done, c)
                        for h in range(GH):
                            mm = pe.matmul(ps[:, 6, cs(h)], kbg[:, c, h, :], S[:, h, :], start=True, stop=True)
                        mm.then_inc(ws_done, 1)
                    if c >= 2:
                        pe.wait_ge(o_copied, c - 1)
                    if c:
                        pe.wait_ge(vn_done, c)
                    new = vnew[:, c % 2] if c else vb[:, 0]
                    for h in range(GH):
                        if c:
                            pe.matmul(ps[:, 4 + c % 2, cs(h)], S[:, h, :], qd[:, h, cs(c)], start=True, stop=False)
                        mm = pe.matmul(ps[:, 4 + c % 2, cs(h)], new[:, h, :], aqk[:, c, h, :], start=not c, stop=True)
                    mm.then_inc(o_done, 1)
                    if c < NCH - 1:
                        for h in range(GH):
                            mm = pe.matmul(ps[:, 2 + c % 2, cs(h)], kdec[:, c, h, :], new[:, h, :], start=True, stop=True)
                        mm.then_inc(ds_done, 1)
                for h in range(GH):
                    if h >= 2:
                        pe.wait_ge(l2_root, 2 * GH + h - 1)
                    stats(1, bank=2 + h % 2)

            def stick_breaking():
                u0, t0, per = U0["sb"], T0["sb"], 6

                def body(s, j):
                    u, t, kind, pair = j * per + (u0 + s), j * per + (t0 + s), s % 3, s // 3
                    bank = (t0 + s) % 2
                    split_ready(u)
                    bank_free(t)
                    if kind < 2:
                        tile(u, u0 + s, 8, ps[:, bank, :], H).then_inc(w_used, 1)
                        return
                    slot = (u0 + s) % 2
                    for c in range(4):
                        for k in range(KD):
                            for n, (w, o) in enumerate(((w_hi, h_hi), (w_hi, h_lo), (w_lo, h_hi))):
                                mm = pe.matmul(ps[:, bank, cs(c)], o[:, k, cs(c)], w[:, slot, k, :],
                                               start=k == 0 and n == 0, stop=k == KD - 1 and n == 2)
                    mm.then_inc(w_used, 1)
                    pe.wait_ge(acc_free, t + 1 + CREDIT)
                    for hh in range(2):
                        a4 = j * 16 + (4 * (2 * pair + hh))
                        rows = slice(64 * hh, 64 * hh + 64)
                        pp = pair % 2
                        pe.wait_ge(sb_att, a4 + 1)
                        for b in range(4):
                            z = ps[:, 2 + b, b * P:SEQ]
                            pe.matmul(z, sbk[rows, pp, cs(b)], sbq[rows, pp, b * P:SEQ], start=True, stop=True)
                            pe.matmul(ps[:, 2 + b, cs(b)], ident[:, :], sbc[:, 2, :], start=False, stop=True,
                                      skip_group_check=True).then_inc(sb_z, 1)
                        pe.wait_ge(sb_l, a4 + 4)
                        for b in range(4):
                            for b2 in range(b, 4):
                                mm = pe.matmul(ps[:, 2 + b, b2 * P:SEQ], sbc[:, 0 if b2 == b else 1, :],
                                               Lb[:, b2, b2 * P:SEQ], start=False, stop=True, skip_group_check=True)
                            mm.then_inc(sb_suf, 1)
                        if hh == 0:
                            pe.wait_ge(val_full, j * 2 + (V0["sb"] + pair - VF["sb"]))
                        for b in range(4):
                            pe.wait_ge(sb_att, a4 + (b + 2))
                            mm = pe.matmul(ps[:, 6, b * P:SEQ], vpad[:, pp, b, hh, :], att[:, b, b * P:SEQ],
                                           start=hh == 0 and b == 0, stop=True, skip_group_check=True)
                        mm.then_inc(sb_o, 1)

                pe.wait_ge(sbc_in, 48)
                unit_loop(pe, 12, per, body, u0=u0)

            def merge():
                u0, t0, per = U0["merge"], T0["merge"], 8

                def body(s, j):
                    u, kind, m = j * per + (u0 + s), s % 4, s // 4
                    t = j * 12 + (t0 + 6 * m + kind)
                    split_ready(u)
                    if kind < 3:
                        bank_free(t)
                        tile(u, u0 + s, 8, ps[:, (t0 + kind) % 2, :], H).then_inc(w_used, 1)
                        return
                    for b in range(3):
                        bank_free(t + b)
                        mm = tile(u, u0 + s, 4, ps[:, (t0 + 3 + b) % 2, :], (y_hi[b], y_lo[b]), w0=4 * b)
                        mm.then_inc(w_used if b == 2 else part_done, 1)

                unit_loop(pe, 32, per, body, u0=u0)

            pe.sem_inc(w_used, CREDIT)
            pe.sem_inc(sq_used, CREDIT)
            pe.wait_ge(consts_in, 32)

            def mix():
                stats()
                plain("ab", 1, v=V0["h_mix"])
                plain("qkv", 12)
                plain("gate", 4)

            def wout():
                plain("wout", KD, xs=(m_hi, m_lo), v=V0["merge"], sums=1)
                stats()

            def ffn1():
                plain("up_a", 16, v=V0["h_ffn"])
                plain("down_a", KD, xs=(f_hi, f_lo), v=V0["up_a"], k_units=2)
                plain("up_b", 16)
                plain("down_b", KD, xs=(f_hi, f_lo), v=V0["up_b"], k_units=2, sums=1)
                stats()

            def s5():
                plain("ssm_in", KD, v=V0["h_mix0"])
                pe.wait_ge(spar_in, 32)
                pe.wait_ge(prep_dve, PREP)
                for b in range(NQ // QB):
                    pe.wait_ge(bp_done[b % 2], b // 2 + 1)
                    b_pow = b_pows[b % 2]
                    if b:
                        pe.wait_ge(lin_done, 4 * b)
                    for n in range(4):
                        for i in range(4):
                            q, comp = 2 * n + i // 2, i % 2
                            tr = pe.transpose(ps[:, 2 + n, cs(i)], b_pow[:, q, comp, :], ident[:, :])
                        tr.then_inc(lt_done, 1)
                    if b:
                        pe.wait_ge(kl_copied, b)
                    for q in range(QB):
                        for gp in range(2):
                            rows, col = slice(64 * gp, 64 * gp + 64), q * GCH
                            for comp in range(2):
                                mm = pe.matmul(ps[:, 6 + gp, col:col + GCH], b_pow[rows, q, comp, :],
                                               c_par(comp, rows, QB * b + q), start=comp == 0, stop=comp == 1)
                    mm.then_inc(kl_done, 1)
                    pe.wait_ge(lin_done, 4 * b + 4)
                    if b == 0:
                        pe.wait_ge(u_in, 16 * SUB)
                    if b:
                        pe.wait_ge(xi_copied, 2 * b)
                    for n in range(2):
                        for i in range(8):
                            q, comp = 4 * n + i // 2, i % 2
                            for gp in range(2):
                                mm = pe.matmul(ps[64 * gp:64 * gp + 64, n, 64 * i:64 * i + 64],
                                               l_in[:, q, comp, 64 * gp:64 * gp + 64],
                                               u_b[:, 2 * (QB * b + q) + gp, :], start=True, stop=True)
                        mm.then_inc(xi_done, 1)
                pe.wait_ge(kl_copied, NQ // QB)

                def lag_blocks(b):
                    for i in range(SUB):
                        mm = pe.matmul(ps[:, 2 + i // 2, 256 * (i % 2):256 * (i % 2) + 256], shifts[:, i, :],
                                       k_lag[:, 256 * b:256 * b + 256], start=True, stop=True)
                        if i % 2:
                            mm.then_inc(tp_done, 1)

                lag_blocks(0)
                for b in range(NQ // QB):
                    pe.wait_ge(tp_copied, 4 * b + 4)
                    if b + 1 < NQ // QB:
                        lag_blocks(b + 1)
                    if b == 0:
                        pe.wait_ge(scan_done, 1)
                    pe.wait_ge(cp_done, b + 1)
                    toep = toeps[b % 2]
                    for n in range(2):
                        if b:
                            pe.wait_ge(y_copied, 2 * b - 1 + n)
                        for q in range(QB):
                            rows, g, out = slice(64 * n, 64 * n + 64), 2 * q + n, ps[:, 6 + n, 64 * q:64 * q + 64]
                            pe.matmul(out, toep[:, g, :, :].rearrange("p i k -> p (i k)"), u_b[:, 2 * QB * b + g, :],
                                      start=True, stop=False)
                            for comp in range(2):
                                mm = pe.matmul(out, c_pows[b % 3][rows, q, comp, :], xp[rows, :, comp, QB * b + q],
                                               start=False, stop=comp == 1)
                        mm.then_inc(y_done, 1)

            def glu():
                plain("glu", 16, v=V0["z"], sums=2)

            def swiglu(l):
                plain(f"gu{l}", 44, v=V0[f"h_ffn{l}"])
                plain(f"dn{l}", KD, xs=(e_hi, e_lo), v=V0[f"gu{l}"], k_units=2, sums=1 - l)

            def head_norm(first):
                pe.wait_ge(rope_in, 16 * 4)

                t = (qh, kh)[first > 0]

                def sums(h, j):
                    pe.wait_ge(hn_sq, j * 2 + (first + h + 1))
                    if h >= 2:
                        pe.wait_ge(hn_root, j * 2 + (first + h - 1))
                    pe.matmul(ps[0:QK, 2 + h % 2, :], mlac[0:QK, 0, 0:QK], sq[0:QK, h % 2, :], start=True, stop=True)\
                      .then_inc(hn_sum, 1)

                def rotated(h, j):
                    pe.wait_ge(hn_scaled, j * 2 + (first + h + 1))
                    pe.wait_ge(hn_done, j * 2 + (first + h + 1))
                    pe.matmul(ps[0:QK, 4 + h % 2, :], mlac[0:QK, 1, 0:QK], one(t, j * 2 + h)[0:QK], start=True,
                              stop=True).then_inc(hn_rot, 1)

                def head(h, j):
                    if h < MH - 1:
                        sums(h + 1, j)
                    if h:
                        rotated(h - 1, j)

                sums(0, 0)
                head_steps(pe, head)
                rotated(MH - 1, 0)

            def mla_q():
                plain("qa", 3, v=V0["h_mix1"])
                stats(3)
                u0, t0, v0 = U0["qb"], T0["qb"], V0["qa"]
                for n in range(4):
                    split_ready(u0 + n)
                    for i in range(4):
                        t = t0 + 4 * n + i
                        bank_free(t)
                        mm = tile(u0 + n, u0 + n, 3, ps[0:QK, t % 2, :], (cq_hi, cq_lo), w0=3 * i, m=QK,
                                  v=v0 if t == t0 else None)
                        mm.then_inc(w_used if i == 3 else part_done, 1)
                head_norm(0)

            def mla_kv():
                plain("kva", 3, v=V0["h_kv"])
                stats(2)
                u0, t0, v0 = U0["kvb"], T0["kvb"], V0["kva"]
                for n in range(4):
                    split_ready(u0 + n)
                    for i in range(4):
                        t = t0 + 6 * n + i
                        bank_free(t)
                        mm = tile(u0 + n, u0 + n, 2, ps[0:64, t % 2, :], (ck_hi, ck_lo), w0=2 * i,
                                  v=v0 if t == t0 else None, m=64)
                        mm.then_inc(part_done, 1)
                    for half in range(2):
                        t = t0 + 6 * n + 4 + half
                        bank_free(t)
                        for c in range(2):
                            out = ps[:, t % 2, 256 * c:256 * c + 256].rearrange("p (h n) -> p h n", h=4)
                            for k in range(2):
                                for m, (w, o) in enumerate(((w_hi, ck_hi), (w_hi, ck_lo), (w_lo, ck_hi))):
                                    mm = pe.matmul(out, o[:, k, cs(2 * half + c)], w[:, (u0 + n) % 2, k:8:2, 64:128],
                                                   start=k == 0 and m == 0, stop=k == 1 and m == 2)
                        mm.then_inc(w_used if half else part_done, 1)
                head_norm(MH)

            def attention():
                pe.wait_ge(hn_done, 2 * MH + CREDIT)
                pe.wait_ge(acc_free, T0["wo"] + CREDIT)

                def scores(i, j):
                    q, k = stage[0:QK, i % 2, :], one(kh, j * 4 + i)[0:QK]
                    pe.wait_ge(at_q, j * 4 + (i + 1))
                    if i >= 2:
                        pe.wait_ge(at_oc, j * 4 + (i - 1))
                    for tb in (0, 2, 1, 3):
                        out = s_block(i, tb)
                        pe.matmul(out, q[:, cs(tb)], k[:, 0:P * tb + P], start=True, stop=True)
                        pe.matmul(out[:, P * tb:P * tb + P], ident[:, :], mlac[:, 2, :], start=False, stop=True,
                                  skip_group_check=True).then_inc(at_s, 1)

                def transposes(n, j, blocks):
                    if n >= 2:
                        pe.wait_ge(at_ptc, j * 18 + (n - 1))
                    for tb, src in blocks:
                        tr = pe.transpose(ps[:, 6 + n % 2, cs(tb)], src, ident[:, :])
                    tr.then_inc(at_pt, 1)

                def output_pair(i, j):
                    pe.wait_ge(at_oc, j * 4 + i)
                    transposes(t_unit(i)[1] - 1, j, [(tb, sq[:, 0, cs(tb)]) for tb in range(4)])

                def head(i, j):
                    if i < MH - 1:
                        scores(i + 1, j)
                    if i % 2 == 0 and i:
                        output_pair(i, j)
                    pe.wait_ge(at_p, j * 16 + (4 * i + 4))
                    total, n = t_unit(i, j)
                    for b in range(4):
                        transposes(n + b, j, [(tb, p_block(i, tb)[:, cs(b)]) for tb in range(b, 4)])
                    pe.wait_ge(at_ptc, total + 4)
                    for tb in range(4):
                        for b in range(tb + 1):
                            mm = pe.matmul(o_block(i, tb), p_t[:, b, cs(tb)],
                                           one_v(b, j * 4 + i), start=b == 0, stop=b == tb)
                    mm.then_inc(at_o, 1)

                def one_v(b, a):
                    return v_t[:, b, a, :] if isinstance(a, int) else \
                        v_t[:, b, bass.ds(a, 1), :].rearrange("p a n -> p (a n)")

                scores(0, 0)
                over_heads(pe, head)
                pe.wait_ge(at_oc, MH)
                transposes(t_unit(MH)[1] - 1, 0, [(tb, sq[:, 0, cs(tb)]) for tb in range(4)])

            def mla_out():
                attention()
                plain("wo", KD, v=V0["attn"], sums=1)

            for step in (mix, delta_rule, stick_breaking, lambda: plain("sc", 12), merge, wout, ffn1, s5, glu,
                         lambda: swiglu(0), mla_q, mla_kv, mla_out, lambda: swiglu(1)):
                step()

        @block.gpsimd
        def _(pool):
            def lo(u, s_u):
                k_n, slot = KTS[s_u], s_u % 2
                pool.wait_ge(hi_done, u + 1)
                pool.tensor_tensor(w_lo[:, slot, 0:k_n, :], w_raw[:, slot, 0:k_n, :], w_hi[:, slot, 0:k_n, :],
                                   ALU.subtract).then_inc(lo_done, 1)

            def lo_value(v, s_v, hi, low):
                pool.wait_ge(val_hi, v + 1)
                pool.tensor_tensor(low, val[:, s_v % 2, :], hi, ALU.subtract).then_inc(val_lo, 1)

            def units(phase, n, work=None, per=2):
                u0 = U0[phase]

                def body(s, j):
                    if u0 + s + 1 < NU:
                        lo(j * per + (u0 + s + 1), u0 + s + 1)
                    if work:
                        work(s, j)
                unit_loop(pool, n, per, body, look=1, u0=u0)

            def values(name, n, hi, low):
                for k in range(n):
                    lo_value(V0[name] + k, V0[name] + k, hi[:, k, :], low[:, k, :])

            def value_units(phase, n, hi, low, per=2, every=1, vals=None):
                v0 = V0[vals or phase]

                def work(s, j):
                    if s % every == every - 1:
                        i = j * (per // every) + s // every
                        lo_value(i + v0, v0 + s // every, one(hi, i), one(low, i))
                units(phase, n, work, per=per)

            pool_link = Chain(pool, pool_chain)
            pool.sem_inc(lo_done, CREDIT)
            pool.sem_inc(val_lo, CREDIT)

            def mix():
                lo(0, 0)
                values("h_mix", KD, h_hi, h_lo)
                units("ab", 1)
                units("qkv", 12)
                units("gate", 4)

            def delta_rule():
                values("gdn", GH, y_hi[0], y_lo[0])
                pool.memset(vpad[:, :, :, :, :], 0.0).then_inc(vpad_zero, 1)

            def wout():
                units("wout", KD)
                values("h_ffn", KD, h_hi, h_lo)

            def ffn1():
                value_units("up_a", 16, f_hi, f_lo)
                units("down_a", 16, per=4)
                value_units("up_b", 16, f_hi, f_lo)
                units("down_b", 16, per=4)
                values("h_mix0", KD, h_hi, h_lo)

            def s5():
                pool.wait_ge(x_ready, 2 * KD)
                pool.memset(xp[:, 0, :, :], 0.0).then_inc(zeros_done, 1)
                units("ssm_in", KD)
                pool.wait_ge(*u_done(U0["ssm_in"] + KD - 1))
                pool.wait_ge(prep_dve, PREP)
                tmp = [pow_tmp[:, n, :].rearrange("p (q i k) -> p q i k", q=QB, i=SUB) for n in range(2)]
                for b in (1, 3):
                    if b == 3:
                        pool.wait_ge(lt_done, 8)
                        pool.wait_ge(kl_done, 2)
                    powers(pool, pool_link, tmp, b_pows[1], b, 0, bbar[:, 0], bbar[:, 1], 0).then_inc(bp_done[1], 1)
                    pool.wait_ge(bp_done[1], b // 2 + 1)
                for b in range(NQ // QB):
                    if b < 2:
                        pool.wait_ge(lt_done, 12 + 4 * b)
                        pool.wait_ge(kl_done, 3 + b)
                    if b == 2:
                        pool.wait_ge(xi_done, 2 * NQ // QB)
                    if b == 3:
                        pool.wait_ge(y_done, 2)
                    powers(pool, pool_link, tmp, c_pows[b % 3], b, 1, par_b(2), par_b(3), 1).then_inc(cp_done, 1)
                    pool.wait_ge(cp_done, b + 1)
                values("z", KD, h_hi, h_lo)

            def glu():
                units("glu", 16)
                values("h_ffn0", KD, h_hi, h_lo)

            def swiglu(l):
                value_units(f"gu{l}", 44, e_hi, e_lo, per=4, every=2)
                units(f"dn{l}", 16, per=4)
                if l == 0:
                    values("h_mix1", KD, h_hi, h_lo)

            def mla_q():
                units("qa", 3)
                values("qa", 3, cq_hi, cq_lo)
                units("qb", 4)
                values("h_kv", KD, h_hi, h_lo)

            def mla_kv():
                units("kva", 3)
                values("kva", 2, ck_hi, ck_lo)
                units("kvb", 4)

            def mla_out():
                with pool.Fori(0, KD // 2) as j:
                    for s in range(2):
                        lo_value(j * 2 + (V0["attn"] + s), V0["attn"] + s, one(h_hi, j * 2 + s), one(h_lo, j * 2 + s))
                units("wo", KD)
                values("h_ffn1", KD, h_hi, h_lo)

            for step in (mix, delta_rule, lambda: value_units("sb", 12, y_hi[1], y_lo[1], per=6, every=3),
                         lambda: value_units("sc", 12, y_hi[2], y_lo[2], per=6, every=3),
                         lambda: value_units("merge", 32, m_hi, m_lo, per=8, every=4), wout, ffn1, s5, glu,
                         lambda: swiglu(0), mla_q, mla_kv, mla_out, lambda: swiglu(1)):
                step()

        @block.scalar
        def _(act):
            link = Chain(act, act_chain)
            squared = [0]

            def hi(u, s_u, j8):
                k_n, slot = KTS[s_u], s_u % 2
                act.wait_ge(raw_in[slot], j8 * 8 + (s_u // 2 + 1) * 16)
                act.wait_ge(w_used, u + 1)
                act.activation(w_hi[:, slot, 0:k_n, :], w_raw[:, slot, 0:k_n, :], ACT.Copy).then_inc(hi_done, 1)

            def hi_value(s_v, dst, wait):
                act.wait_ge(*wait)
                act.activation(dst, val[:, s_v % 2, :], ACT.Copy).then_inc(val_hi, 1)

            def units(phase, n, work=None, per=2, chain=None, ops=0):
                u0 = U0[phase]

                def body(s, j):
                    if u0 + s + 1 < NU:
                        hi(j * per + (u0 + s + 1), u0 + s + 1, j * per)
                    if work:
                        work(s, j)
                unit_loop(act, n, per, body, look=1, u0=u0, chain=chain, ops=ops)

            def squares(tiles, ready=None):
                for k, src in enumerate(tiles):
                    if ready:
                        act.wait_ge(*ready(k))
                    act.wait_ge(sq_used, squared[0] + 1)
                    act.activation(sq[:, squared[0] % 2, :], src, ACT.Square).then_inc(sq_full, 1)
                    squared[0] += 1

            def square_of(src, g, i, ready):
                act.wait_ge(*ready)
                act.wait_ge(sq_used, i + (squared[0] + 1))
                act.activation(sq[:, (squared[0] + g) % 2, :], one(src, i), ACT.Square).then_inc(sq_full, 1)

            def square_units(phase, src, ready, per=2, every=1, also=None):
                def work(s, j):
                    if also:
                        also(s, j)
                    if s % every == every - 1:
                        i = j * (per // every) + s // every
                        square_of(src, s // every, i, ready(i))
                units(phase, KD * every, work, per=per)
                squared[0] += KD

            def all_tiles(t, n=KD):
                return [t[:, k, :] for k in range(n)]

            def root(n=D, bank=7):
                act.wait_ge(sq_used, squared[0] + CREDIT)
                act.preload_act_table_set(LN_EXP)
                link(act.activation(rs[:, :], ps[:, bank, :], ACT.Ln, scale=1.0 / n, bias=pc("eps")))
                act.activation(rs[:, :], rs[:, :], ACT.Exp, scale=-0.5).then_inc(root_done, 1)

            def values(name, n, dst):
                for k in range(n):
                    v = V0[name] + k
                    hi_value(v, dst[:, k, :], (val_full, v + 1 - VF[name]))

            def head_norms(tiles, l0, n, ready=None):
                def rooted(j):
                    act.wait_ge(sq_used, first + j + 1 + CREDIT)
                    if l0 + j >= 2:
                        act.wait_ge(l2_done, l0 + j - 1)
                    link(act.activation(stage[:, j % 2, :], ps[:, 2 + j % 2, :], ACT.Ln, scale=1.0 / n, bias=pc("eps")))
                    act.activation(stage[:, j % 2, :], stage[:, j % 2, :], ACT.Exp, scale=-0.5).then_inc(l2_root, 1)
                first = squared[0]
                act.preload_act_table_set(LN_EXP)
                for j, src in enumerate(tiles):
                    squares([src], (lambda k: ready) if ready else None)
                    if j:
                        rooted(j - 1)
                rooted(len(tiles) - 1)

            def silu_tiles(phase, n, dst, full):
                g0 = G0[phase]

                def work(s, j):
                    act.wait_ge(*full(s, j))
                    act.activation(one(dst, j * 2 + s), stage[:, (g0 + s) % 2, :], ACT.Silu).then_inc(stage_free, 1)
                act.preload_act_table(ACT.Silu)
                units(phase, n, work)

            def value_units(phase, n, dst, wait, per=2, every=1):
                v0 = V0[phase]

                def work(s, j):
                    if s % every == every - 1:
                        i = j * (per // every) + s // every
                        hi_value(v0 + s // every, one(dst, i), wait(s, j))
                units(phase, n, work, per=per)

            def mix():
                hi(0, 0, 0)
                squares(all_tiles(x))
                root()
                values("h_mix", KD, h_hi)
                units("ab", 1)
                act.wait_ge(ab_abs, 1)
                act.activation(gcol[0:8, 0, 0:1], pc("a_log", rows=slice(0, 8)), ACT.Exp)
                link(act.activation(stage[0:8, 0, :], stage[0:8, 0, :], ACT.Exp))
                act.activation(stage[0:8, 0, :], stage[0:8, 0, :], ACT.Ln, bias=1.0).then_inc(ab_exp, 1)
                act.activation(b_rows[:, :], stage[0:8, 1, :], ACT.Sigmoid).then_inc(ab_sig, 1)
                silu_tiles("qkv", 12, qkv, lambda s, j: (stage_full, j * 2 + (s + 1)))
                silu_tiles("gate", 4, gsil, lambda s, j: (acc_free, j * 2 + (T0["gate"] + s + 1 + CREDIT)))

            def delta_rule():
                head_norms(all_tiles(qkv, 2 * GH), 0, 1)
                act.wait_ge(kdc_sub, 1)
                act.activation(egc[:, :, :], gcol[:, :, 0:GH], ACT.Exp)
                link(act.activation(kdc[:, :, :], kdc[:, :, :], ACT.Exp))
                act.activation(glc[:, :, :], g_last, ACT.Exp).then_inc(cols_exp, 1)
                for h in range(GH):
                    act.activation(qd[:, h, :], Gb[:, h, :], ACT.Exp).then_inc(qd_exp, 1)
                for c in range(NCH):
                    act.wait_ge(dmin_done, c + 1)
                    act.activation(stage[:, c % 2, :], stage[:, c % 2, :], ACT.Exp).then_inc(dec_done, 1)
                for n in range(NCH * LEVELS):
                    act.wait_ge(x_done, n + 1)
                    if n >= NCH:
                        act.wait_ge(dtu_done, n - NCH + 1)
                    else:
                        act.wait_ge(akk_done, NCH)
                    act.activation(Xm[:, n % NCH].rearrange("p h n -> p (h n)"), ps[:, 2 + n % 2, :], ACT.Copy)\
                       .then_inc(xs_done, 1)
                for c in range(NCH):
                    act.wait_ge(uw_done, c + 1)
                    act.activation(kbg[:, c].rearrange("p h n -> p (h n)"), ps[:, 3 + 2 * (c % 2), :], ACT.Copy)\
                       .then_inc(w_copied, 1)
                head_norms(all_tiles(o_t, GH), 2 * GH, P, (o_copied, NCH))
                values("gdn", GH, y_hi[0])
                for n in range(3):
                    act.dma_start(sbc[:, n, :], t_const[:, (CIX["negtri"] + n) * P:(CIX["negtri"] + n + 1) * P])\
                       .then_inc(sbc_in, 16)

            def stick_breaking():
                u0, v0 = U0["sb"], V0["sb"]

                def work(s, j):
                    if s % 3 < 2:
                        return
                    pair = s // 3
                    for hh in range(2):
                        a4 = j * 16 + 4 * (2 * pair + hh)
                        for b in range(4):
                            e = ez[:, b, b * P:SEQ]
                            act.wait_ge(sb_z, a4 + (b + 1))
                            link(act.activation(e, ps[:, 2 + b, b * P:SEQ], ACT.Abs))
                            link(act.activation(e, e, ACT.Exp, scale=-1.0))
                            act.activation(e, e, ACT.Ln, bias=1.0).then_inc(sb_ln, 1)
                        for b in range(4):
                            act.wait_ge(sb_suf, a4 + (b + 1))
                            act.activation(att[:, b, b * P:SEQ], ps[:, 2 + b, b * P:SEQ], ACT.Exp).then_inc(sb_att, 1)
                    v = j * 2 + (v0 + pair)
                    hi_value(v0 + pair, one(y_hi[1], j * 2 + pair), (val_full, v + 1 - VF["sb"]))

                act.sem_inc(sb_att, 1)
                act.preload_act_table_set(LN_EXP)
                units("sb", 12, work, per=6, chain=link, ops=32)

            def merge():
                t0, g0 = T0["merge"], G0["merge"]

                def work(s, j):
                    kind, m = s % 4, s // 4
                    if kind < 3:
                        act.wait_ge(acc_free, j * 12 + (t0 + 6 * m + kind + 1 + CREDIT))
                        act.activation(gsig[:, kind, :], stage[:, (g0 + 3 * m + kind) % 2, :], ACT.Sigmoid)\
                           .then_inc(stage_free, 1)
                        return
                    v = V0["merge"] + m
                    hi_value(v, one(m_hi, j * 2 + m), (val_full, j * 2 + (v + 1 - VF["merge"])))

                act.preload_act_table(ACT.Sigmoid)
                units("merge", 32, work, per=8)

            def norm_of(src, ready=None):
                squares(all_tiles(src), ready)
                root()

            def wout():
                square_units("wout", y, lambda i: (acc_free, i + (T0["wout"] + 1 + CREDIT)))
                root()
                norm_of(x, lambda k: (x_ready, k + 1))
                values("h_ffn", KD, h_hi)

            def s5_steps(s, j):
                if s == 5:
                    act.wait_ge(prep_dve, 1)
                    act.activation(sm[:, 1, :], sm[:, 1, :], ACT.Exp).then_inc(prep_act, 1)
                    link(act.activation(sm[:, 3, :], sm[:, 3, :], ACT.Sin))
                    act.activation(sm[:, 4, :], sm[:, 4, :], ACT.Sin).then_inc(prep_act, 1)

            def ffn1():
                for half in "ab":
                    up = "up_" + half
                    if half == "a":
                        act.dma_start(spar[:, :], t_ssm).then_inc(spar_in, 16)
                        act.dma_start(shifts[:, :, :].rearrange("p n c -> p (n c)"),
                                      t_const[:, CIX["shift0"] * P:(CIX["shift0"] + SUB) * P]).then_inc(spar_in, 16)
                    value_units(up, 16, f_hi, lambda s, j: (val_full, j * 2 + (V0[up] + s + 1 - VF[up])))
                    if half == "a":
                        act.wait_ge(spar_in, 32)
                        act.activation(sm[:, 0, :], spar[:, 2 * NQ:3 * NQ], ACT.Exp).then_inc(prep_act, 1)
                        units("down_a", 16, s5_steps, per=16)
                square_units("down_b", ysum, lambda i: (acc_free, i + (T0["down_b"] + 1 + CREDIT)), per=4, every=2)
                root()
                norm_of(x, lambda k: (x_ready, KD + k + 1))
                values("h_mix0", KD, h_hi)

            def s5():
                units("ssm_in", KD)
                for b in range(NQ // QB):
                    for n in range(4):
                        act.wait_ge(lt_done, 4 * b + n + 1)
                        if b and n == 0:
                            act.wait_ge(xi_done, 2 * b)
                        act.activation(l_in[:, 2 * n:2 * n + 2].rearrange("p q c n -> p (q c n)"), ps[:, 2 + n, :],
                                       ACT.Copy).then_inc(lin_done, 1)
                    act.wait_ge(kl_done, b + 1)
                    act.activation(k_lag[:, 256 * b:256 * b + 256].rearrange("p (q g k) -> p g q k", q=QB, g=2),
                                   ps[:, 6:8, 0:P].rearrange("p g (q k) -> p g q k", k=GCH), ACT.Copy).then_inc(kl_copied, 1)
                for b in range(NQ // QB):
                    for n in range(4):
                        act.wait_ge(tp_done, 4 * b + n + 1)
                        if b > 1 and n == 0:
                            act.wait_ge(y_done, 2 * b - 2)
                        act.activation(toeps[b % 2][:, :, 2 * n:2 * n + 2, :],
                                       ps[:, 2 + n, :].rearrange("p (i g k) -> p g i k", i=2, k=GCH), ACT.Copy)\
                           .then_inc(tp_copied, 1)
                for r in range(SUB):
                    if r == 0:
                        act.wait_ge(y_copied, 2 * NQ // QB)
                    act.dma_start(t_scratch_y.rearrange("(g k) j c -> j k g c", k=GCH)[r], u_b[GCH * r:GCH * r + GCH, :, :])\
                       .then_inc(y_out, 16)
                act.wait_ge(y_out, 16 * SUB)
                act.dma_start(y_t[:, :, :], t_scratch_y.rearrange("(t p) j c -> p t (j c)", p=P)).then_inc(y_in, 16)
                for k in range(KD):
                    v, g = V0["z"] + k, G0["z"] + k
                    act.wait_ge(stage_full, 12 + k + 1)
                    act.wait_ge(val_lo, v + 1)
                    act.activation(val[:, v % 2, :].rearrange("p (c j) -> p j c", j=SUB),
                                   stage[:, g % 2, :].rearrange("p (j c) -> p j c", j=SUB), ACT.Gelu_apprx_tanh)\
                       .then_inc(stage_free, 1)
                    hi_value(v, h_hi[:, k, :], (stage_free, g + 1 + CREDIT))

            def glu():
                t0, g0 = T0["glu"], G0["glu"]

                def work(s, j):
                    if s % 2 == 0:
                        act.wait_ge(acc_free, j * 4 + (t0 + s + 1 + CREDIT))
                        act.activation(sgl[:, s // 2 % 2, :], stage[:, (g0 + s // 2) % 2, :], ACT.Sigmoid)\
                           .then_inc(stage_free, 1)
                act.preload_act_table(ACT.Sigmoid)
                square_units("glu", x, lambda i: (x_ready, i + (2 * KD + 1)), per=4, every=2, also=work)
                root()
                values("h_ffn0", KD, h_hi)

            def swiglu(l):
                gu, dn = f"gu{l}", f"dn{l}"
                t0, g0, v0 = T0[gu], G0[gu], V0[gu]

                def work(s, j):
                    m = s // 2
                    act.wait_ge(acc_free, j * 4 + (t0 + s + 1 + CREDIT))
                    if s % 2 == 0:
                        act.activation(sgate[:, m % 2, :], stage[:, (g0 + m) % 2, :], ACT.Silu).then_inc(stage_free, 1)
                    else:
                        act.activation(one(e_hi, j * 2 + m), val[:, (v0 + m) % 2, :], ACT.Copy).then_inc(val_hi, 1)
                act.preload_act_table(ACT.Silu)
                units(gu, 44, work, per=4)
                if l:
                    units(dn, 16, per=4)
                else:
                    square_units(dn, x, lambda i: (acc_free, i + (T0[dn] + 1 + CREDIT)), per=4, every=2)
                    root()
                    values("h_mix1", KD, h_hi)

            def head_norm(first):
                t = (qh, kh)[first > 0]
                act.preload_act_table_set(LN_EXP)

                def square(h, j):
                    if first:
                        act.wait_ge(kr_copied, j * 2 + (h + 1))
                    if h >= 2:
                        act.wait_ge(hn_sum, j * 2 + (first + h - 1))
                    act.activation(sq[0:QK, h % 2, :], one(t, j * 2 + h)[0:QK], ACT.Square).then_inc(hn_sq, 1)

                def head(h, j):
                    if h < MH - 1:
                        square(h + 1, j)
                    r = stage[0:QK, h % 2, :]
                    act.wait_ge(hn_sum, j * 2 + (first + h + 1))
                    if h >= 2:
                        act.wait_ge(hn_scaled, j * 2 + (first + h - 1))
                    link(act.activation(r, ps[0:QK, 2 + h % 2, :], ACT.Ln, bias=pc("eps", rows=slice(0, QK))))
                    act.activation(r, r, ACT.Exp, scale=-0.5).then_inc(hn_root, 1)

                square(0, 0)
                head_steps(act, head, chain=link, ops=2)

            def mla_q():
                act.dma_start(pos_i[0:QK, :], t_pos).then_inc(rope_in, 16)
                for n, name in enumerate(("blk96", "rot", "mlamask")):
                    act.dma_start(mlac[:, n, :], t_const[:, CIX[name] * P:(CIX[name] + 1) * P]).then_inc(rope_in, 16)
                act.wait_ge(trig_arg, 1)
                act.activation(sin_t[0:QK, :], sin_t[0:QK, :], ACT.Sin).then_inc(trig_done, 1)
                act.activation(cos_t[0:QK, :], cos_t[0:QK, :], ACT.Sin).then_inc(trig_done, 1)
                units("qa", 3)
                squares(all_tiles(cq_raw, 3), lambda k: (acc_free, T0["qa"] + k + 1 + CREDIT))
                root(384)
                values("qa", 3, cq_hi)
                units("qb", 4)
                act.wait_ge(acc_free, T0["qb"] + MH + CREDIT)
                head_norm(0)
                values("h_kv", KD, h_hi)

            def mla_kv():
                units("kva", 3)
                squares(all_tiles(ck_raw, 2), lambda k: (acc_free, T0["kva"] + k + 1 + CREDIT))
                root(256)
                values("kva", 2, ck_hi)
                act.wait_ge(acc_free, T0["kva"] + 3 + CREDIT)
                for h in range(MH):
                    act.activation(kh[64:QK, h, :], kr_raw[64:QK, :], ACT.Copy).then_inc(kr_copied, 1)
                units("kvb", 4)
                act.wait_ge(acc_free, T0["kvb"] + 24 + CREDIT)
                head_norm(MH)

            def mla_out():
                act.wait_ge(hn_done, 2 * MH + CREDIT)

                def queries(i, j):
                    if i >= 2:
                        act.wait_ge(at_s, j * 16 + 4 * (i - 1))
                    act.activation(stage[0:QK, i % 2, :], one(qh, j * 4 + i)[0:QK], ACT.Copy).then_inc(at_q, 1)

                def exps(i, j):
                    act.wait_ge(at_max, j * 4 + (i + 1))
                    if i >= 2:
                        act.wait_ge(at_pt, t_unit(i - 1, j)[0])
                        act.wait_ge(at_oc, j * 4 + (i - 1))
                    for tb in range(4):
                        act.activation(p_block(i, tb), s_block(i, tb), ACT.Exp, bias=nmax[:, i % 2, tb:tb + 1],
                                       scale=QK ** -0.5, accum_out=psums[:, i % 2, tb:tb + 1]).then_inc(at_p, 1)

                def output_pair(i, j):
                    total, n = t_unit(i, j)
                    p = i // 2 - 1
                    act.wait_ge(at_pt, total)
                    act.wait_ge(val_lo, j * 2 + (V0["attn"] + p + 1))
                    act.activation(val[:, (V0["attn"] + p) % 2, :], ps[:, 6 + (n - 1) % 2, :], ACT.Copy).then_inc(at_ot, 1)
                    act.activation(one(h_hi, j * 2 + p), ps[:, 6 + (n - 1) % 2, :], ACT.Copy).then_inc(at_ptc, 1)
                    act.wait_ge(at_ot, j * 2 + (p + 1))
                    act.wait_ge(at_ptc, total)
                    act.sem_inc(val_hi, 1)

                def head(i, j):
                    total, n = t_unit(i, j)
                    if i % 2 == 0 and i:
                        output_pair(i, j)
                    for b in range(4):
                        act.wait_ge(at_pt, total + (b + 1))
                        act.activation(p_t[:, b, b * P:SEQ], ps[:, 6 + (n + b) % 2, b * P:SEQ], ACT.Copy)\
                           .then_inc(at_ptc, 1)
                    if i < MH - 2:
                        queries(i + 2, j)
                    if i < MH - 1:
                        exps(i + 1, j)

                queries(0, 0)
                queries(1, 0)
                exps(0, 0)
                over_heads(act, head)
                output_pair(MH, 0)
                square_units("wo", x, lambda i: (acc_free, i + (T0["wo"] + 1 + CREDIT)))
                root()
                values("h_ffn1", KD, h_hi)

            act.sem_inc(stage_free, CREDIT)
            act.wait_ge(params_in, 16)
            act.wait_ge(x_in, 16)
            sc_wait = lambda s, j: (val_full, j * 2 + (V0["sc"] + s // 3 + 1 - VF["sc"]))
            for step in (mix, delta_rule, stick_breaking, lambda: value_units("sc", 12, y_hi[2], sc_wait, per=6, every=3),
                         merge, wout, ffn1, s5, glu, lambda: swiglu(0), mla_q, mla_kv, mla_out,
                         lambda: swiglu(1)):
                step()

        @block.vector
        def _(dve):
            link = Chain(dve, dve_chain)
            roots, x_steps = [0], [0]

            def copy_tile(dst, bank, u):
                dve.wait_ge(*u_done(u))
                dve.tensor_copy(dst, ps[:, bank, :]).then_inc(acc_free, 1)

            def inverse_root():
                roots[0] += 1
                dve.wait_ge(root_done, roots[0])

            def put_value(v, s_v, f, counted=True):
                dve.wait_ge(val_lo, v + 1)
                return f(val[:, s_v % 2, :])

            def normed(name, gain, src=x, n=KD):
                for k in range(n):
                    v = V0[name] + k
                    put_value(v, v, lambda o: dve.scalar_tensor_tensor(
                        out=o, in0=src[:, k, :], scalar=pc(gain, k), in1=rs[:, :], op0=ALU.mult, op1=ALU.mult)
                        .then_inc(val_full, 1))

            def post_norm(src, gain):
                inverse_root()
                for k in range(KD):
                    link(dve.scalar_tensor_tensor(out=src[:, k, :], in0=src[:, k, :], scalar=pc(gain, k), in1=rs[:, :],
                                                  op0=ALU.mult, op1=ALU.mult))
                    dve.tensor_tensor(x[:, k, :], x[:, k, :], src[:, k, :], ALU.add).then_inc(x_ready, 1)
                    x_steps[0] += 1
                dve.wait_ge(x_ready, x_steps[0])

            def mix():
                inverse_root()
                normed("h_mix", "mix_pre")
                dve.wait_ge(*u_done(U0["ab"]))
                dve.tensor_scalar(stage[0:8, 1, :], ps[0:8, T0["ab"] % 2, :], pc("dt_bias", rows=slice(0, 8)), None,
                                  ALU.add).then_inc(acc_free, 1)
                dve.wait_ge(acc_free, T0["ab"] + 1 + CREDIT)
                z = stage[0:8, 1, :]
                dve.scalar_tensor_tensor(out=stage[0:8, 0, :], in0=z, scalar=-1.0, in1=z, op0=ALU.mult, op1=ALU.min)\
                   .then_inc(ab_abs, 1)
                dve.wait_ge(ab_exp, 1)
                link(dve.scalar_tensor_tensor(out=stage[0:8, 0, :], in0=z, scalar=0.0, in1=stage[0:8, 0, :],
                                              op0=ALU.max, op1=ALU.add))
                link(dve.tensor_scalar(stage[0:8, 0, :], stage[0:8, 0, :], gcol[0:8, 0, 0:1], -1.0, ALU.mult, ALU.mult))
                link(dve.memset(rs[0:8, :], 1.0))
                link(dve.memset(rs[0:8, :].rearrange("p (c n) -> p c n", n=CHUNK)[:, :, 0:1], 0.0))
                dve.tensor_tensor_scan(g_rows[:, :], rs[0:8, :], stage[0:8, 0, :], 0.0, ALU.mult, ALU.add)\
                   .then_inc(g_ready, 1)
                dve.wait_ge(g_ready, 1)
                dve.wait_ge(ab_sig, 1)
                link(dve.memset(cbuf[:, :, 0:3], 0.0))
                u0, t0, g0 = U0["qkv"], T0["qkv"], G0["qkv"]

                def conv(s, j):
                    b = (g0 + s) % 2
                    copy_tile(cbuf[:, b, 3:3 + SEQ], (t0 + s) % 2, j * 2 + (u0 + s))
                    dve.wait_ge(acc_free, j * 2 + (t0 + s + 1 + CREDIT))
                    dve.wait_ge(stage_free, j * 2 + (g0 + s + 1))
                    acc = stage[:, b, :]
                    link(dve.tensor_scalar(acc, cbuf[:, b, 0:SEQ], pc("conv_qkv", j * 8 + 4 * s), None, ALU.mult))
                    for tap in range(1, 4):
                        ins = dve.scalar_tensor_tensor(out=acc, in0=cbuf[:, b, tap:tap + SEQ],
                                                       scalar=pc("conv_qkv", j * 8 + (4 * s + tap)), in1=acc,
                                                       op0=ALU.mult, op1=ALU.add)
                        if tap < 3:
                            link(ins)
                    ins.then_inc(stage_full, 1)
                unit_loop(dve, 12, 2, conv, chain=link, ops=6, u0=u0)

                def gate(s, j):
                    dve.wait_ge(stage_free, j * 2 + (G0["gate"] + s + 1))
                    copy_tile(stage[:, (G0["gate"] + s) % 2, :], (T0["gate"] + s) % 2, j * 2 + (U0["gate"] + s))
                unit_loop(dve, 4, 2, gate, u0=U0["gate"])

            def head_scale(l, src, scale):
                dve.wait_ge(l2_root, l + 1)
                return dve.scalar_tensor_tensor(out=src, in0=src, scalar=scale, in1=stage[:, l % 2, :],
                                                op0=ALU.mult, op1=ALU.mult)

            def delta_rule():
                dve.wait_ge(gc_in, 16)
                for l in range(2 * GH):
                    head_scale(l, qkv[:, l, :], P ** -0.5 if l < GH else 1.0).then_inc(l2_done, 1)
                for m in range(2 * GH):
                    dve.wait_ge(bc_done, m + 1)
                    dve.tensor_copy((Bb if m % 2 else Gb)[:, m // 2, :], ps[:, 4 + m % 2, :]).then_inc(bc_copied, 1)
                dve.wait_ge(bc_copied, 2 * GH)
                dve.wait_ge(cols_done, 1)
                link(dve.tensor_copy(gcol[:, :, :].rearrange("p c n -> p (c n)"), ps[:, 6, 0:32]))
                link(dve.tensor_copy(bcol[:, :, :].rearrange("p c n -> p (c n)"), ps[:, 6, 32:64]))
                dve.tensor_tensor(kdc[:, :, :], g_last, gcol[:, :, 0:GH], ALU.subtract).then_inc(kdc_sub, 1)
                dve.wait_ge(cols_exp, 1)
                link(dve.tensor_tensor(egc[:, :, :], egc[:, :, :], bcol[:, :, GH:2 * GH], ALU.mult))
                for h in range(GH):
                    dve.wait_ge(qd_exp, h + 1)
                    link(dve.tensor_tensor(qd[:, h, :], qd[:, h, :], qkv[:, h, :], ALU.mult))

                def heads(t):
                    return t.rearrange("p (h n) -> p h n", h=GH)

                def per_head(col):
                    return col.unsqueeze(2).to_broadcast([P, GH, P])

                for c in range(NCH):
                    dve.wait_ge(tok_done, c + 1)
                    dve.tensor_tensor(kbg[:, c], heads(ps[:, 2, :]), per_head(egc[:, c, :]), ALU.mult)
                    dve.tensor_tensor(kdec[:, c], heads(ps[:, 2, :]), per_head(kdc[:, c, :]), ALU.mult)
                    dve.tensor_tensor(vb[:, c], heads(ps[:, 3, :]), per_head(bcol[:, c, GH:2 * GH]), ALU.mult)\
                       .then_inc(tok_used, 1)
                    for h in range(GH):
                        ins = dve.tensor_scalar(stage[:, c % 2, cs(h)], Gb[:, h, cs(c)], gcol[:, c, h:h + 1], 0.0,
                                                ALU.subtract, ALU.min)
                    ins.then_inc(dmin_done, 1)
                    dve.wait_ge(dec_done, c + 1)
                    dve.wait_ge(kq_done, c + 1)
                    dec = heads(stage[:, c % 2, :])
                    mask = [gc[:, n, :].unsqueeze(1).to_broadcast([P, GH, P]) for n in range(2)]
                    link(dve.tensor_tensor(aqk[:, c], heads(ps[:, 5, :]), dec, ALU.mult))
                    dve.tensor_tensor(aqk[:, c], aqk[:, c], mask[0], ALU.mult)
                    link(dve.tensor_tensor(akk[:, c], heads(ps[:, 4, :]), dec, ALU.mult))
                    link(dve.tensor_tensor(akk[:, c], akk[:, c], mask[1], ALU.mult))
                    dve.tensor_tensor(akk[:, c], akk[:, c], Bb[:, :, cs(c)], ALU.mult).then_inc(akk_done, 1)
                dve.wait_ge(akk_done, NCH)
                eye = ident[:, :].unsqueeze(1).to_broadcast([P, NCH * GH, P])
                for t in (Tm, Um):
                    link(dve.tensor_copy(t[:, :, :, :].rearrange("p c h n -> p (c h) n"), eye))

                def mask_level(n):
                    c = n % NCH
                    if n >= NCH:
                        dve.wait_ge(x_done, n - NCH + 1)
                    lev = gc[:, 2 + n // NCH, :].unsqueeze(1).to_broadcast([P, GH, P])
                    dve.tensor_tensor(AM[:, c], akk[:, c], lev, ALU.mult).then_inc(am_done, 1)

                def update(n):
                    c, b = n % NCH, 4 + 2 * (n % 2)
                    dve.wait_ge(dtu_done, n + 1)
                    if n < NCH * (LEVELS - 1):
                        dve.tensor_tensor(Tm[:, c], Tm[:, c], heads(ps[:, b, :]), ALU.subtract)
                    dve.tensor_tensor(Um[:, c], Um[:, c], heads(ps[:, b + 1, :]), ALU.subtract).then_inc(tu_done, 1)

                mask_level(0)
                for n in range(NCH * LEVELS):
                    if n + 1 < NCH * LEVELS:
                        mask_level(n + 1)
                    if n:
                        update(n - 1)
                update(NCH * LEVELS - 1)
                for c in range(NCH):
                    dve.wait_ge(uw_done, c + 1)
                    dve.tensor_copy(vb[:, c], heads(ps[:, 2 + 2 * (c % 2), :])).then_inc(u_copied, 1)
                dve.wait_ge(u_copied, NCH)
                for c in range(NCH):
                    if c:
                        dve.wait_ge(ws_done, c)
                        if c >= 3:
                            dve.wait_ge(ds_done, c - 1)
                        dve.tensor_tensor(vnew[:, c % 2], vb[:, c], heads(ps[:, 6, :]), ALU.subtract).then_inc(vn_done, 1)
                    dve.wait_ge(o_done, c + 1)
                    dve.tensor_copy(o_t[:, :, cs(c)], heads(ps[:, 4 + c % 2, :])).then_inc(o_copied, 1)
                    if c == NCH - 1:
                        break
                    dve.wait_ge(ds_done, c + 1)
                    if c == 0:
                        dve.tensor_copy(S[:, :, :], heads(ps[:, 2, :])).then_inc(s_done, 1)
                    else:
                        for h in range(GH):
                            ins = dve.scalar_tensor_tensor(out=S[:, h, :], in0=S[:, h, :], scalar=glc[:, c, h:h + 1],
                                                           in1=ps[:, 2 + c % 2, cs(h)], op0=ALU.mult, op1=ALU.add)
                        ins.then_inc(s_done, 1)
                    dve.wait_ge(s_done, c + 1)
                for h in range(GH):
                    ins = head_scale(2 * GH + h, o_t[:, h, :], pc("gdn_norm"))
                    ins.then_inc(l2_done, 1)
                    dve.wait_ge(l2_done, 2 * GH + h + 1)
                    put_value(V0["gdn"] + h, V0["gdn"] + h, lambda o: dve.tensor_tensor(
                        o, o_t[:, h, :], gsil[:, h, :], ALU.mult).then_inc(val_full, 1))

            def stick_breaking():
                u0, t0, v0 = U0["sb"], T0["sb"], V0["sb"]

                def body(s, j):
                    u, bank, kind, pair = j * 6 + (u0 + s), (t0 + s) % 2, s % 3, s // 3
                    pp = pair % 2
                    dve.wait_ge(*u_done(u))
                    if kind == 0:
                        dve.tensor_scalar(sbq[:, pp, :], ps[:, bank, :], 0.125, None, ALU.mult).then_inc(acc_free, 1)
                        return
                    if kind == 1:
                        dve.tensor_copy(sbk[:, pp, :], ps[:, bank, :]).then_inc(acc_free, 1)
                        return
                    vt = ps[:, bank, :].rearrange("p (c n) -> p c n", c=4)
                    dve.tensor_copy(vpad[:, pp, :, 0, 0:64], vt[:, :, 0:64])
                    dve.tensor_copy(vpad[:, pp, :, 1, 64:128], vt[:, :, 64:128]).then_inc(acc_free, 1)
                    for hh in range(2):
                        a4 = j * 16 + 4 * (2 * pair + hh)
                        for b in range(4):
                            dve.wait_ge(sb_ln, a4 + (b + 1))
                            dve.scalar_tensor_tensor(out=Lb[:, b, b * P:SEQ], in0=ps[:, 2 + b, b * P:SEQ], scalar=0.0,
                                                     in1=ez[:, b, b * P:SEQ], op0=ALU.max, op1=ALU.add).then_inc(sb_l, 1)
                    dve.wait_ge(sb_o, j * 4 + (2 * pair + 2))
                    v = j * 2 + (v0 + pair)
                    put_value(v, v0 + pair, lambda o: dve.tensor_copy(o, ps[:, 6, :]).then_inc(val_full, 1))

                dve.wait_ge(vpad_zero, 1)
                unit_loop(dve, 12, 6, body, u0=u0)

            def short_conv():
                u0, t0, v0 = U0["sc"], T0["sc"], V0["sc"]
                link(dve.memset(scx[:, :, 0:2], 0.0))

                def body(s, j):
                    u, bank, kind, n = j * 6 + (u0 + s), (t0 + s) % 2, s % 3, s // 3
                    b = n % 2
                    dve.wait_ge(*u_done(u))
                    if kind == 0:
                        dve.tensor_copy(scc[:, b, :], ps[:, bank, :]).then_inc(acc_free, 1)
                    elif kind == 1:
                        dve.wait_ge(acc_free, j * 6 + (t0 + s + CREDIT))
                        dve.tensor_tensor(scx[:, b, 2:2 + SEQ], scc[:, b, :], ps[:, bank, :], ALU.mult).then_inc(acc_free, 1)
                        dve.wait_ge(acc_free, j * 6 + (t0 + s + 1 + CREDIT))
                        acc = sct[:, b, :]
                        link(dve.tensor_scalar(acc, scx[:, b, 0:SEQ], pc("conv_sc", j * 6 + 3 * n), None, ALU.mult))
                        for tap in (1, 2):
                            link(dve.scalar_tensor_tensor(out=acc, in0=scx[:, b, tap:tap + SEQ],
                                                          scalar=pc("conv_sc", j * 6 + (3 * n + tap)), in1=acc,
                                                          op0=ALU.mult, op1=ALU.add))
                    else:
                        v = j * 2 + (v0 + n)
                        dve.tensor_tensor(sct[:, b, :], sct[:, b, :], ps[:, bank, :], ALU.mult).then_inc(acc_free, 1)
                        dve.wait_ge(acc_free, j * 6 + (t0 + s + 1 + CREDIT))
                        put_value(v, v0 + n, lambda o: dve.tensor_copy(o, sct[:, b, :]).then_inc(val_full, 1))
                unit_loop(dve, 12, 6, body, chain=link, ops=6, u0=u0)

            def merge():
                u0, t0, g0, v0 = U0["merge"], T0["merge"], G0["merge"], V0["merge"]

                def body(s, j):
                    u, kind, m = j * 8 + (u0 + s), s % 4, s // 4
                    t, g = j * 12 + (t0 + 6 * m + 3), j * 6 + (g0 + 3 * m)
                    if kind < 3:
                        dve.wait_ge(stage_free, g + (kind + 1))
                        copy_tile(stage[:, (g0 + 3 * m + kind) % 2, :], (t0 + kind) % 2, u)
                        return
                    for b in range(3):
                        if b < 2:
                            dve.wait_ge(part_done, j * 4 + (2 * m + b + 1))
                        else:
                            dve.wait_ge(*u_done(u))
                        dve.wait_ge(stage_free, g + (b + 1 + CREDIT))
                        dve.tensor_tensor(mt[:, min(b, 1), :], gsig[:, b, :], ps[:, (t0 + 3 + b) % 2, :], ALU.mult)\
                           .then_inc(acc_free, 1)
                        dve.wait_ge(acc_free, t + (b + 1 + CREDIT))
                        if b == 1:
                            link(dve.tensor_tensor(mt[:, 0, :], mt[:, 0, :], mt[:, 1, :], ALU.add))
                    put_value(j * 2 + (v0 + m), v0 + m, lambda o: dve.tensor_tensor(
                        o, mt[:, 0, :], mt[:, 1, :], ALU.add).then_inc(val_full, 1))

                unit_loop(dve, 32, 8, body, chain=link, ops=2, u0=u0)

            def tiles(phase, n, f, k_units=1):
                u0, t0 = U0[phase], T0[phase]

                def body(s, j):
                    dve.wait_ge(*u_done(j * (2 * k_units) + (u0 + (s + 1) * k_units - 1)))
                    f(s, j, ps[:, (t0 + s) % 2, :]).then_inc(acc_free, 1)
                unit_loop(dve, n, 2, body, u0=u0)

            def wout():
                tiles("wout", KD, lambda s, j, acc: dve.tensor_copy(one(y, j * 2 + s), acc))
                post_norm(y, "mix_post")
                inverse_root()
                normed("h_ffn", "ffn_pre")

            def ffn1():
                for half in "ab":
                    up, down = "up_" + half, "down_" + half

                    u0, t0, v0 = U0[up], T0[up], V0[up]

                    def relu_squared(s, j):
                        r = relu[:, s % 2, :]
                        dve.wait_ge(*u_done(j * 2 + (u0 + s)))
                        dve.tensor_scalar(r, ps[:, (t0 + s) % 2, :], 0.0, None, ALU.max).then_inc(acc_free, 1)
                        dve.wait_ge(acc_free, j * 2 + (t0 + s + 1 + CREDIT))
                        put_value(j * 2 + (v0 + s), v0 + s,
                                  lambda o: dve.tensor_tensor(o, r, r, ALU.mult).then_inc(val_full, 1))
                    unit_loop(dve, 16, 2, relu_squared, u0=u0)
                    if half == "a":
                        for k in range(KD):
                            dve.wait_ge(*u_done(U0[down] + 2 * k + 1))
                            dve.tensor_copy(ysum[:, k, :], ps[:, (T0[down] + k) % 2, :]).then_inc(acc_free, 1)
                            if k in s5_parts:
                                s5_parts[k]()
                    else:
                        tiles(down, KD, lambda s, j, acc: dve.tensor_tensor(
                            one(ysum, j * 2 + s), one(ysum, j * 2 + s), acc, ALU.add), k_units=2)
                post_norm(ysum, "ffn_post")
                inverse_root()
                normed("h_mix0", "mix0")

            dve.sem_inc(acc_free, CREDIT)
            dve.wait_ge(params_in, 16)
            dve.wait_ge(x_in, 16)
            def tt(out, a, b, op):
                link(dve.tensor_tensor(out, a, b, op))

            def reduced_angle(out, src, turns, scratch, add):
                n = scratch
                link(dve.tensor_scalar(n, src, 1.0 / TWO_PI, turns, ALU.mult, ALU.add))
                link(dve.tensor_scalar(n, n, MAGIC, MAGIC, ALU.add, ALU.subtract))
                link(dve.scalar_tensor_tensor(out=out, in0=n, scalar=-C1, in1=src, op0=ALU.mult, op1=ALU.add))
                link(dve.scalar_tensor_tensor(out=out, in0=n, scalar=-C2, in1=out, op0=ALU.mult, op1=ALU.add))
                link(dve.scalar_tensor_tensor(out=out, in0=n, scalar=-C3, in1=out, op0=ALU.mult, op1=ALU.add))
                link(dve.tensor_scalar(out, out, add, PI_BELOW, ALU.add, ALU.min))
                return dve.tensor_scalar(out, out, -PI_BELOW, None, ALU.max)

            def cmul(re, im, ar, ai, br, bi, t1, t2):
                link(dve.tensor_tensor(t1, ar, br, ALU.mult))
                link(dve.tensor_tensor(t2, ai, bi, ALU.mult))
                link(dve.tensor_tensor(re, t1, t2, ALU.subtract))
                link(dve.tensor_tensor(t1, ar, bi, ALU.mult))
                link(dve.tensor_tensor(t2, ai, br, ALU.mult))
                link(dve.tensor_tensor(im, t1, t2, ALU.add))

            def f(n):
                return sm[:, n, :]

            lr, li = spar[:, 0:NQ], spar[:, NQ:2 * NQ]

            def s5_angles():
                dve.wait_ge(prep_act, 1)
                link(dve.tensor_tensor(f(1), lr, f(0), ALU.mult))
                link(dve.tensor_tensor(f(2), li, f(0), ALU.mult))
                link(reduced_angle(f(3), f(2), 0.0, f(5), 0.0))
                reduced_angle(f(4), f(2), 0.25, f(5), TWO_PI / 4).then_inc(prep_dve, 1)

            def doubled(t, at0, scratch):
                for n in (1, 2, 4):
                    w = [t[:, c, at0 + n - 1, :].unsqueeze(1).to_broadcast([P, n, NQ]) for c in range(2)]
                    new, old = slice(at0 + n, at0 + 2 * n), slice(at0, at0 + n)
                    cmul(t[:, 0, new, :], t[:, 1, new, :], t[:, 0, old, :], t[:, 1, old, :], w[0], w[1],
                         *(sm[:, c:c + n, :] for c in scratch))

            def s5_powers():
                dve.wait_ge(prep_act, 3)
                link(dve.memset(pw[:, 0, 0, :], 1.0))
                link(dve.memset(pw[:, 1, 0, :], 0.0))
                tt(pw[:, 0, 1, :], f(1), f(4), ALU.mult)
                tt(pw[:, 1, 1, :], f(1), f(3), ALU.mult)
                doubled(pw, 1, (4, 8))

            def s5_chunk_powers():
                for c in range(2):
                    link(dve.tensor_copy(pa[:, c, 0, :], pw[:, c, SUB, :]))
                doubled(pa, 0, (4, 8))

            def s5_factor():
                ar, ai = pw[:, 0, 1, :], pw[:, 1, 1, :]
                link(dve.tensor_scalar(f(0), ar, -1.0, None, ALU.add))
                tt(f(1), lr, lr, ALU.mult)
                tt(f(2), li, li, ALU.mult)
                tt(f(1), f(1), f(2), ALU.add)
                link(dve.reciprocal(f(1), f(1)))
                tt(f(2), f(0), lr, ALU.mult)
                tt(f(3), ai, li, ALU.mult)
                tt(f(2), f(2), f(3), ALU.add)
                tt(f(2), f(2), f(1), ALU.mult)
                tt(f(3), ai, lr, ALU.mult)
                tt(f(4), f(0), li, ALU.mult)
                tt(f(3), f(3), f(4), ALU.subtract)
                tt(f(3), f(3), f(1), ALU.mult)

            def s5_inputs():
                for n, im in ((10, pw[:, 1, SUB, :]), (8, pa[:, 1, 7, :])):
                    link(dve.tensor_scalar(f(n), im, -1.0, None, ALU.mult))
                    link(dve.tensor_copy(f(n + 1), im))
                wide = lambda v: v.unsqueeze(2).to_broadcast([P, NQ, GCH])
                s1, s2 = (stage[:, n, :].rearrange("p (q k) -> p q k", k=GCH) for n in range(2))
                cmul(bbar[:, 0], bbar[:, 1], wide(f(2)), wide(f(3)), par_b(0), par_b(1), s1, s2)
                dve.tensor_scalar(par_b(3), par_b(3), -1.0, None, ALU.mult).then_inc(prep_dve, PREP - 1)
                dve.wait_ge(prep_dve, PREP)

            s5_parts = {1: s5_angles, 3: s5_powers, 4: s5_chunk_powers, 5: s5_factor, 6: s5_inputs}

            def scan():
                n = 8
                xs = xp[:, :, :, :].rearrange("p (s i) m q -> p s i m q", i=n)
                t = [scan_tmp[:, c, :] for c in range(2)]
                t1, t2 = (v[:, 0:n * 2 * NQ].rearrange("p (s m q) -> p s m q", s=n, m=2) for v in t)
                wide = lambda v: v.unsqueeze(1).to_broadcast([P, n, NQ])
                a8 = pw[:, 0, SUB, :].unsqueeze(1).unsqueeze(1).to_broadcast([P, n, 2, NQ])
                for i in range(1, n):
                    now, nxt = xs[:, :, i - 1], xs[:, :, i]
                    dve.tensor_tensor(t1, now, a8, ALU.mult)
                    dve.tensor_tensor(t2[:, :, 0, :], now[:, :, 1, :], wide(f(10)), ALU.mult)
                    link(dve.tensor_tensor(t2[:, :, 1, :], now[:, :, 0, :], wide(f(11)), ALU.mult))
                    link(dve.tensor_tensor(nxt, nxt, t1, ALU.add))
                    link(dve.tensor_tensor(nxt, nxt, t2, ALU.add))
                a64 = pa[:, 0, n - 1, :].unsqueeze(1).to_broadcast([P, 2, NQ])
                for s in range(1, n):
                    now, nxt = xs[:, s - 1, n - 1], xs[:, s, n - 1]
                    dve.tensor_tensor(sm[:, 0:2, :], now, a64, ALU.mult)
                    dve.tensor_tensor(sm[:, 2, :], now[:, 1, :], f(8), ALU.mult)
                    link(dve.tensor_tensor(sm[:, 3, :], now[:, 0, :], f(9), ALU.mult))
                    link(dve.tensor_tensor(nxt, nxt, sm[:, 0:2, :], ALU.add))
                    link(dve.tensor_tensor(nxt, nxt, sm[:, 2:4, :], ALU.add))
                m = n - 1
                t1, t2 = (v[:, 0:m * m * NQ].rearrange("p (s i q) -> p s i q", s=m, i=m) for v in t)
                for comp in range(2):
                    out = xs[:, 1:n, 0:m, comp, :]
                    for v, w in ((t1, 0), (t2, 1)):
                        carry = xs[:, 0:m, m, comp ^ w, :].unsqueeze(2).to_broadcast([P, m, m, NQ])
                        ins = dve.tensor_tensor(v, pa[:, w, 0:m, :].unsqueeze(1).to_broadcast([P, m, m, NQ]), carry,
                                                ALU.mult)
                    link(ins)
                    link(dve.tensor_tensor(out, out, t1, ALU.add))
                    ins = dve.tensor_tensor(out, out, t2, ALU.add if comp else ALU.subtract)
                    if comp == 0:
                        link(ins)
                ins.then_inc(scan_done, 1)

            def s5():
                tiles("ssm_in", KD, lambda s, j, acc: dve.tensor_copy(
                    one(u_t, j * 2 + s).rearrange("p (j c) -> p j c", j=SUB), acc.rearrange("p (c j) -> p j c", j=SUB)))

                tmp = [t[:, :, :].rearrange("p a n -> p (a n)").rearrange("p (q i k) -> p q i k", q=QB, i=SUB)
                       for t in (stage, sq)]

                powers(dve, link, tmp, b_pow, 0, 0, bbar[:, 0], bbar[:, 1], 0).then_inc(bp_done[0], 1)
                dve.wait_ge(zeros_done, 1)
                for b in range(NQ // QB):
                    if b == 0:
                        dve.wait_ge(bp_done[0], 1)
                        dve.wait_ge(lt_done, 4)
                        dve.wait_ge(kl_done, 1)
                        powers(dve, link, tmp, b_pow, 2, 0, bbar[:, 0], bbar[:, 1], 0).then_inc(bp_done[0], 1)
                    for n in range(2):
                        dve.wait_ge(xi_done, 2 * b + n + 1)
                        q0 = QB * b + 4 * n
                        dve.tensor_copy(xp[:, 1:NSUB, :, q0:q0 + 4].rearrange("p c m q -> p q m c"),
                                        ps[:, n, :].rearrange("p (q m c) -> p q m c", q=4, m=2)[:, :, :, 0:NSUB - 1])\
                           .then_inc(xi_copied, 1)
                dve.wait_ge(xi_copied, 2 * NQ // QB)
                scan()
                for b in range(NQ // QB):
                    for n in range(2):
                        dve.wait_ge(y_done, 2 * b + n + 1)
                        dve.tensor_copy(u_b[:, 16 * b + n:16 * b + 16:2, :],
                                        ps[:, 6 + n, :].rearrange("p (q c) -> p q c", q=QB)).then_inc(y_copied, 1)
                dve.wait_ge(y_in, 16)
                for k in range(KD):
                    g = G0["z"] + k
                    dve.wait_ge(stage_free, g + 1)
                    dve.scalar_tensor_tensor(out=stage[:, g % 2, :], in0=u_t[:, k, :], scalar=pc("d_skip", k),
                                             in1=y_t[:, k, :], op0=ALU.mult, op1=ALU.add).then_inc(stage_full, 1)

            def glu():
                u0, t0, g0 = U0["glu"], T0["glu"], G0["glu"]

                def body(s, j):
                    m, t = s // 2, j * 4 + (t0 + s)
                    if s % 2 == 0:
                        dve.wait_ge(stage_free, j * 2 + (g0 + m + 1))
                        copy_tile(stage[:, (g0 + m) % 2, :], (t0 + s) % 2, j * 4 + (u0 + s))
                        return
                    dve.wait_ge(*u_done(j * 4 + (u0 + s)))
                    dve.wait_ge(stage_free, j * 2 + (g0 + m + 1 + CREDIT))
                    r = sgl[:, m % 2, :]
                    dve.tensor_tensor(r, r, ps[:, (t0 + s) % 2, :], ALU.mult).then_inc(acc_free, 1)
                    dve.wait_ge(acc_free, t + (1 + CREDIT))
                    dve.tensor_tensor(one(x, j * 2 + m), one(x, j * 2 + m), r, ALU.add).then_inc(x_ready, 1)
                unit_loop(dve, 16, 4, body, u0=u0)
                x_steps[0] += KD
                inverse_root()
                normed("h_ffn0", "ffn0")

            def add_to_x(phase, k_units=1):
                tiles(phase, KD, lambda s, j, acc: dve.tensor_tensor(one(x, j * 2 + s), one(x, j * 2 + s), acc, ALU.add),
                      k_units=k_units)

            def swiglu(l):
                gu = f"gu{l}"
                u0, t0, g0, v0 = U0[gu], T0[gu], G0[gu], V0[gu]

                def body(s, j):
                    m = s // 2
                    if s % 2 == 0:
                        dve.wait_ge(stage_free, j * 2 + (g0 + m + 1))
                        copy_tile(stage[:, (g0 + m) % 2, :], (t0 + s) % 2, j * 4 + (u0 + s))
                        return
                    dve.wait_ge(*u_done(j * 4 + (u0 + s)))
                    dve.wait_ge(stage_free, j * 2 + (g0 + m + 1 + CREDIT))
                    dve.wait_ge(val_lo, j * 2 + (v0 + m + 1))
                    dve.tensor_tensor(val[:, (v0 + m) % 2, :], sgate[:, m % 2, :], ps[:, (t0 + s) % 2, :], ALU.mult)\
                       .then_inc(acc_free, 1)
                unit_loop(dve, 44, 4, body, u0=u0)
                add_to_x(f"dn{l}", k_units=2)
                if l == 0:
                    inverse_root()
                    link(dve.tensor_copy(rs_keep[:, :], rs[:, :]))
                    normed("h_mix1", "mix1")

            def head_norm(first):
                t, gain = ((qh, pc("q_head", rows=slice(0, QK))), (kh, pc("k_head", rows=slice(0, QK))))[first > 0]

                def rotated(h, j):
                    v = one(t, j * 2 + h)[0:QK]
                    dve.wait_ge(hn_rot, j * 2 + (first + h + 1))
                    dve.wait_ge(hn_done, j * 2 + (first + h + CREDIT))
                    link(dve.tensor_tensor(rs[0:QK, :], ps[0:QK, 4 + h % 2, :], sin_t[0:QK, :], ALU.mult))
                    link(dve.tensor_tensor(v, v, cos_t[0:QK, :], ALU.mult))
                    dve.tensor_tensor(v, v, rs[0:QK, :], ALU.add).then_inc(hn_done, 1)

                def head(h, j):
                    v = one(t, j * 2 + h)[0:QK]
                    dve.wait_ge(hn_root, j * 2 + (first + h + 1))
                    dve.scalar_tensor_tensor(out=v, in0=v, scalar=gain, in1=stage[0:QK, h % 2, :], op0=ALU.mult, op1=ALU.mult)\
                       .then_inc(hn_scaled, 1)
                    if h:
                        rotated(h - 1, j)

                head_steps(dve, head, chain=link, ops=4)
                rotated(MH - 1, 0)

            def mla_q():
                dve.wait_ge(rope_in, 16 * 4)
                rows = slice(0, QK)
                link(dve.tensor_copy(ang[rows, :], pos_i[rows, :]))
                link(dve.tensor_scalar(ang[rows, :], ang[rows, :], pc("inv_freq", rows=rows), None, ALU.mult))
                link(reduced_angle(sin_t[rows, :], ang[rows, :], 0.0, mt_f[rows, :], 0.0))
                reduced_angle(cos_t[rows, :], ang[rows, :], 0.25, mt_f[rows, :], TWO_PI / 4).then_inc(trig_arg, 1)
                dve.sem_inc(hn_done, CREDIT)
                tiles("qa", 3, lambda s, j, acc: dve.tensor_copy(one(cq_raw, j * 2 + s), acc))
                inverse_root()
                normed("qa", "q_a", src=cq_raw, n=3)
                u0, t0 = U0["qb"], T0["qb"]
                for h in range(MH):
                    if h % 4 < 3:
                        dve.wait_ge(part_done, 16 + 3 * (h // 4) + h % 4 + 1)
                    else:
                        dve.wait_ge(*u_done(u0 + h // 4))
                    dve.tensor_copy(qh[0:QK, h, :], ps[0:QK, (t0 + h) % 2, :]).then_inc(acc_free, 1)
                dve.wait_ge(trig_done, 2)
                head_norm(0)
                dve.wait_ge(hn_done, MH + CREDIT)
                link(dve.tensor_copy(rs[:, :], rs_keep[:, :]))
                normed("h_kv", "kv_in")

            def mla_kv():
                u0, t0 = U0["kva"], T0["kva"]
                for n in range(3):
                    dve.wait_ge(*u_done(u0 + n))
                    dst, rows = (ck_raw[:, n, :], slice(0, P)) if n < 2 else (kr_raw[64:QK, :], slice(64, QK))
                    dve.tensor_copy(dst, ps[rows, (t0 + n) % 2, :]).then_inc(acc_free, 1)
                inverse_root()
                normed("kva", "kv_a", src=ck_raw, n=2)
                u0, t0 = U0["kvb"], T0["kvb"]
                for n in range(4):
                    for i in range(6):
                        t = t0 + 6 * n + i
                        if i < 5:
                            dve.wait_ge(part_done, 16 + 12 + 5 * n + i + 1)
                        else:
                            dve.wait_ge(*u_done(u0 + n))
                        if i < 4:
                            ins = dve.tensor_copy(kh[0:64, 4 * n + i, :], ps[0:64, t % 2, :])
                        else:
                            c = 2 * (i - 4)
                            ins = dve.tensor_copy(v_t[:, c:c + 2, 4 * n:4 * n + 4, :],
                                                  ps[:, t % 2, :].rearrange("p (c h n) -> p c h n", c=2, h=4))
                        ins.then_inc(acc_free, 1)
                head_norm(MH)

            def mla_out():
                def maxima(i, j):
                    for tb, n in ((0, 2), (2, 2), (1, 3), (3, 4)):
                        dve.wait_ge(at_s, j * 16 + (4 * i + n))
                        ins = dve.tensor_reduce(nmax[:, i % 2, tb:tb + 1], s_block(i, tb), AX_X, ALU.max)
                    link(ins)
                    dve.tensor_scalar(nmax[:, i % 2, :], nmax[:, i % 2, :], -(QK ** -0.5), None, ALU.mult).then_inc(at_max, 1)

                def head(i, j):
                    if i < MH - 1:
                        maxima(i + 1, j)
                    dve.wait_ge(at_p, j * 16 + (4 * i + 4))
                    link(dve.reciprocal(psums[:, i % 2, :], psums[:, i % 2, :]))
                    dve.wait_ge(at_o, j * 4 + (i + 1))
                    dve.tensor_tensor(sq[:, 0, :].rearrange("p (c n) -> p c n", c=4)[:, :, 64 * (i % 2):64 * (i % 2) + 64],
                                      ps[:, 3 * (i % 2) + 2, 256:512].rearrange("p (c n) -> p c n", c=4),
                                      psums[:, i % 2, :].unsqueeze(2).to_broadcast([P, 4, 64]), ALU.mult).then_inc(at_oc, 1)

                maxima(0, 0)
                over_heads(dve, head, chain=link, ops=8)
                add_to_x("wo")
                inverse_root()
                normed("h_ffn1", "ffn1")

            for step in (mix, delta_rule, stick_breaking, short_conv, merge, wout, ffn1, s5, glu, lambda: swiglu(0),
                         mla_q, mla_kv, mla_out, lambda: swiglu(1)):
                step()


def _consts():
    import numpy as np

    i, j = np.arange(P)[:, None], np.arange(P)[None, :]
    z = np.zeros((P, P), np.float32)
    c = {"ident": i == j, "ones": z == 0, "incl": j >= i, "strict": j > i}
    for lev in range(LEVELS):
        s = 1 << lev
        c[f"lev{lev}"] = (i // (2 * s) == j // (2 * s)) & (j // s % 2 == 1) & (i // s % 2 == 0)
    for r in range(8):
        c[f"sel{r}"] = (i == r) & (j >= 0)
    c["negtri"] = -1.0 * (i >= j)
    c["negones"] = z - 1
    c["sbmask"] = NEG * (i >= j)
    c["mlamask"] = NEG * (j > i)
    for r in range(SUB):
        c[f"shift{r}"] = (i % GCH == j % GCH) & (i // GCH == r - (SUB - 1) + j // GCH)
    blk = z.copy()
    blk[0:64, 0:64] = 1 / 64
    blk[64:96, 64:96] = 1 / 32
    c["blk96"] = blk
    rot = z.copy()
    for r in range(16):
        rot[80 + r, 64 + r] = -1
        rot[64 + r, 80 + r] = 1
    c["rot"] = rot
    return np.ascontiguousarray(np.concatenate([np.asarray(c[n], np.float32) for n in CONST], 1))


def _cols(v, n):
    return v.reshape(n, P).T


def kernel(**a):
    import numpy as np
    import concourse.bacc as _bacc
    from concourse.bass_utils import run_bass_kernel_spmd as _run

    a = {k: np.asarray(v) for k, v in a.items()}
    f32 = np.float32

    def pad_cols(cols):
        out = np.zeros((cols.shape[0], P), f32)
        out[:, 0:cols.shape[1]] = cols
        return out

    def tiles(w, starts):
        return [w[:, c:c + P] for c in starts]

    w_in, wb = a["w_in"][0], a["w_branch"][0]
    o_gate, o_a, o_sb, o_sc, o_g = 1536, 2048, 2056, 3592, 5128
    units = [pad_cols(w_in[:, o_a:o_a + 8])]
    units += tiles(w_in, range(0, 1536, P)) + tiles(w_in, range(o_gate, o_a, P))
    for p in range(SB_PAIRS):
        units += tiles(w_in, [o_sb + 512 * n + P * p for n in range(3)])
    for j in range(4):
        units += tiles(w_in, [o_sc + 1024 + P * j, o_sc + P * j, o_sc + 512 + P * j])
    for m in range(KD):
        units += tiles(w_in, [o_g + D * b + P * m for b in range(3)])
        units.append(np.concatenate([wb[b][:, P * m:P * m + P] for b in range(3)], 0))
    units += tiles(a["w_out"][0], range(0, D, P))
    for half in range(2):
        h0 = half * FF1_HALF * P
        units += tiles(a["w_ff1"][0], range(h0, h0 + FF1_HALF * P, P))
        for m in range(KD):
            for q in range(2):
                units.append(a["w_ff2"][0][h0 + q * 1024:h0 + (q + 1) * 1024, P * m:P * m + P])
    units += tiles(a["ssm_w_in_2"][0], range(0, D, P))
    for m in range(KD):
        units += tiles(a["ssm_w_glu_2"][0], [D + P * m, P * m])

    def feed_forward(l):
        gu, dn, out = a["ffn_w_gate_up_2"][l], a["ffn_w_down_2"][l], []
        for m in range(F2T):
            out += tiles(gu, [P * m, F2T * P + P * m])
        for m in range(KD):
            for q in range(2):
                out.append(dn[q * 1408:(q + 1) * 1408, P * m:P * m + P])
        return out

    units += feed_forward(0)
    units += tiles(a["mla_w_q_a_2"][0], range(0, 384, P))
    wq = a["mla_w_q_b_2"][0]
    for u in range(4):
        units.append(np.concatenate([pad_cols(wq[:, QK * h:QK * h + QK]) for h in range(4 * u, 4 * u + 4)], 0))
    wkva = a["mla_w_kv_a_2"]
    rope = np.zeros((D, P), f32)
    rope[:, 64:96] = wkva[:, 256:288]
    units += tiles(wkva, (0, P)) + [rope]
    wkv = a["mla_w_kv_b_2"]
    for u in range(4):
        units.append(np.concatenate([wkv[:, P * h:P * h + P] for h in range(4 * u, 4 * u + 4)], 0))
    units += tiles(a["mla_w_o_2"][0], range(0, D, P)) + feed_forward(1)
    assert len(units) == NU
    w = np.zeros((NU, P, 12 * P), f32)
    for u, t in enumerate(units):
        k = t.shape[0] // P
        assert k == KTS[u], (u, k)
        w[u, :, 0:k * P] = t.reshape(k, P, P).transpose(1, 0, 2).reshape(P, k * P)

    par = np.zeros((P, NPAR), f32)

    def put(name, block):
        block = np.asarray(block)
        block = block.reshape(block.shape[0], -1)
        par[0:block.shape[0], PCOL[name]:PCOL[name] + block.shape[1]] = block

    for name, v in [("mix_pre", a["norm_mix_pre"][0]), ("mix_post", a["norm_mix_post"][0]),
                    ("ffn_pre", a["norm_ffn_pre"][0]), ("ffn_post", a["norm_ffn_post"][0]),
                    ("mix0", a["mix_norm_2"][0]), ("mix1", a["mix_norm_2"][1]), ("ffn0", a["ffn_norm_2"][0]),
                    ("ffn1", a["ffn_norm_2"][1]), ("kv_in", a["kv_in_norm_2"]), ("d_skip", a["ssm_d_2"][0])]:
        put(name, _cols(v, KD))
    put("conv_qkv", a["conv_qkv_w"][0].reshape(4, 12, P).transpose(2, 1, 0))
    put("conv_sc", a["conv_sc_w"][0].reshape(3, 4, P).transpose(2, 1, 0))
    put("gdn_norm", a["gdn_norm_w"][0][:, None])
    put("a_log", a["gdn_a_log"][0][:, None])
    put("dt_bias", a["gdn_dt_bias"][0][:, None])
    put("kv_a", _cols(a["mla_kv_a_norm_2"], 2))
    put("q_a", _cols(a["mla_q_a_norm_2"][0], 3))
    put("k_head", np.concatenate([a["mla_k_nope_norm_2"], a["mla_k_rope_norm_2"]])[:, None])
    put("q_head", np.concatenate([a["mla_q_nope_norm_2"][0], a["mla_q_rope_norm_2"][0]])[:, None])
    inv = (10000.0 ** (-np.arange(0, 32, 2, dtype=f32) / f32(32))).astype(f32)
    put("inv_freq", np.concatenate([np.zeros(64, f32), inv, inv])[:, None])
    put("eps", np.full((P, 1), EPS, f32))

    def states(v):
        v = v.reshape((NQ, 2 * NST) + v.shape[2:])
        return np.moveaxis(v, 1, 0).reshape(P, -1)

    log_step = np.broadcast_to(a["ssm_log_step_2"][0][:, None], (GROUPS, NST))
    ssm = np.concatenate([states(a["ssm_lambda_re_2"][0]), states(a["ssm_lambda_im_2"][0]), states(log_step),
                          states(a["ssm_b_re_2"][0]), states(a["ssm_b_im_2"][0]),
                          states(a["ssm_c_re_2"][0].transpose(0, 2, 1)),
                          states(a["ssm_c_im_2"][0].transpose(0, 2, 1))], 1)
    arrays = {
        "x": a["x"][0].T.reshape(KD, P, SEQ).transpose(1, 0, 2),
        "par": par, "const": _consts(), "w": w,
        "pos": np.broadcast_to(a["positions_2"].reshape(1, SEQ), (QK, SEQ)), "ssm": ssm,
    }
    nc = _bacc.Bacc("TRN2", target_bir_lowering=False, num_devices=1)
    args = []
    for name in arrays:
        arrays[name] = np.ascontiguousarray(arrays[name])
        args.append(nc.dram_tensor(f"in_{name}", arrays[name].shape, mybir.dt.from_np(arrays[name].dtype),
                                   kind="ExternalInput").ap())
    out = nc.dram_tensor("out_t", (P, KD, SEQ), F32, kind="ExternalOutput").ap()
    scratch = [nc.dram_tensor(f"scratch_{n}", (D, SUB, NSUB), F32, kind="Internal").ap() for n in "uy"]
    build(nc, *args, out, *scratch)
    r = _run(nc, [{f"in_{k}": v for k, v in arrays.items()}], core_ids=[0])
    got = r.results[0]["out_t"]
    return got.transpose(1, 0, 2).reshape(D, SEQ).T.reshape(1, SEQ, D)
```
